# Optimizing a Trainium2 kernel written in Bass

```python
import jax, jax.numpy as jnp
from jax import lax
import numpy as np

D_MODEL = 1024
BATCH = 1
SEQ = 512
DEPTH = 1

HEAD_DIM = 64
NSA_HEADS = 8
NSA_KV_GROUPS = 2
FOX_HEADS = 8
ROT_DIM = HEAD_DIM // 4
ROPE_THETA = 500000.0
CMP_BLOCK = 32
CMP_STRIDE = 16
SEL_BLOCK = 64
N_SEL = 8
WINDOW = 512
Q_BLOCK = 128
N_EXPERTS = 32
TOP_K = 4
D_FF = D_MODEL
SWIGLU_ALPHA = 1.702
SWIGLU_LIMIT = 7.0
MOE_BLOCK = 128
NORM_EPS = 1e-6
NEG = -1e30
FORCE_BONUS = 1e4

NSA_Q = NSA_HEADS * HEAD_DIM
NSA_KV = NSA_KV_GROUPS * HEAD_DIM
NSA_GATE = NSA_HEADS * 3
FOX_W = FOX_HEADS * HEAD_DIM
IN_SIZES = [NSA_Q, NSA_KV, NSA_KV, NSA_KV, NSA_KV, NSA_KV, NSA_KV, NSA_GATE, FOX_W, FOX_W, FOX_W, FOX_HEADS, D_MODEL, D_MODEL]
IN_COLS = sum(IN_SIZES)
IN_SPLITS = [int(v) for v in np.cumsum(IN_SIZES)[:-1]]

kernel_name = 'hybrid_nsa_fox_moe_block'

def rms_norm(x, g):
    xf = x.astype(jnp.float32)
    y = xf * lax.rsqrt(jnp.mean(xf * xf, axis=-1, keepdims=True) + NORM_EPS)
    return (y * g.astype(jnp.float32)).astype(x.dtype)

def masked_softmax(logits, mask):
    l = jnp.where(mask, logits.astype(jnp.float32), NEG)
    return jnp.where(mask, jax.nn.softmax(l, axis=-1), 0.0)

def partial_rope(x, positions):
    freqs = ROPE_THETA ** (-jnp.arange(0, ROT_DIM, 2, dtype=jnp.float32) / ROT_DIM)
    ang = positions.astype(jnp.float32)[..., None] * freqs
    cos, sin = jnp.cos(ang)[:, :, None, :], jnp.sin(ang)[:, :, None, :]
    xr = x[..., :ROT_DIM].astype(jnp.float32)
    x1, x2 = xr[..., :ROT_DIM // 2], xr[..., ROT_DIM // 2:]
    rot = jnp.concatenate([x1 * cos - x2 * sin, x2 * cos + x1 * sin], axis=-1)
    return jnp.concatenate([rot.astype(x.dtype), x[..., ROT_DIM:]], axis=-1)

def compress_blocks(kv, pos_emb, w1, w2):
    B, S, G, DH = kv.shape
    n_c = (S - CMP_BLOCK) // CMP_STRIDE + 1
    idx = np.arange(n_c)[:, None] * CMP_STRIDE + np.arange(CMP_BLOCK)[None, :]
    blk = kv[:, idx] + pos_emb[None, None, :, None, :]
    blk = jnp.moveaxis(blk, 3, 2).reshape(B, n_c, G, CMP_BLOCK * DH)
    return jax.nn.gelu(blk @ w1) @ w2

def nsa_mixer(q, k_c, v_c, k_s, v_s, k_w, v_w, gate_logits, positions, cmp_pos_emb, cmp_w1, cmp_w2):
    B, S = q.shape[:2]
    G, HPG, DH = NSA_KV_GROUPS, NSA_HEADS // NSA_KV_GROUPS, HEAD_DIM
    scale = DH ** -0.5
    n_q = S // Q_BLOCK
    q = q.reshape(B, S, NSA_HEADS, DH)
    k_c, v_c, k_s, v_s, k_w, v_w = [a.reshape(B, S, G, DH) for a in (k_c, v_c, k_s, v_s, k_w, v_w)]
    t = jnp.arange(S)

    kcmp = compress_blocks(k_c, cmp_pos_emb[0], cmp_w1[0], cmp_w2[0])
    vcmp = compress_blocks(v_c, cmp_pos_emb[1], cmp_w1[1], cmp_w2[1])
    n_c = kcmp.shape[1]
    cmp_end = jnp.arange(n_c) * CMP_STRIDE + CMP_BLOCK - 1
    cmp_mask = cmp_end[None, :] <= t[:, None]
    qg = q.reshape(B, S, G, HPG, DH)
    logits = jnp.einsum('bsghd,bcgd->bghsc', qg, kcmp) * scale
    p_cmp = masked_softmax(logits, cmp_mask)
    o_c = jnp.einsum('bghsc,bcgd->bsghd', p_cmp.astype(vcmp.dtype), vcmp).reshape(B, S, NSA_HEADS, DH)

    n_sb = S // SEL_BLOCK
    n_sel = min(N_SEL, n_sb)
    ci = np.arange(n_c)[:, None] * CMP_STRIDE
    sj = np.arange(n_sb)[None, :] * SEL_BLOCK
    overlap = jnp.asarray(((ci < sj + SEL_BLOCK) & (ci + CMP_BLOCK > sj)).astype(np.float32))
    imp = jnp.einsum('bghsc,cj->bgsj', p_cmp, overlap)
    blk_id = jnp.arange(n_sb)[None, :]
    cur = (t // SEL_BLOCK)[:, None]
    valid = blk_id * SEL_BLOCK <= t[:, None]
    forced = (blk_id == 0) | (blk_id == cur) | (blk_id == cur - 1)
    score = jnp.where(forced, imp + FORCE_BONUS, jnp.where(valid, imp, NEG))
    _, sel_idx = lax.top_k(score, n_sel)

    q_r = partial_rope(q, positions).reshape(B, S, G, HPG, DH)
    k_s = partial_rope(k_s, positions)
    k_w = partial_rope(k_w, positions)
    q_blk = jnp.moveaxis(q_r.reshape(B, n_q, Q_BLOCK, G, HPG, DH), 1, 0)

    ks_blk = k_s.reshape(B, n_sb, SEL_BLOCK, G, DH).transpose(0, 3, 1, 2, 4)
    vs_blk = v_s.reshape(B, n_sb, SEL_BLOCK, G, DH).transpose(0, 3, 1, 2, 4)
    idx_blk = jnp.moveaxis(sel_idx.reshape(B, G, n_q, Q_BLOCK, n_sel), 2, 0)
    bi = jnp.arange(B)[:, None, None, None]
    gi = jnp.arange(G)[None, :, None, None]

    def sel_step(args):
        qb, ib, i = args
        tq = i * Q_BLOCK + jnp.arange(Q_BLOCK)
        kg = ks_blk[bi, gi, ib]
        vg = vs_blk[bi, gi, ib]
        lg = jnp.einsum('bqghd,bgqnkd->bgqhnk', qb, kg) * scale
        kpos = ib[..., None] * SEL_BLOCK + jnp.arange(SEL_BLOCK)
        mask = (kpos <= tq[:, None, None])[:, :, :, None].reshape(B, G, Q_BLOCK, 1, n_sel * SEL_BLOCK)
        p = masked_softmax(lg.reshape(B, G, Q_BLOCK, HPG, n_sel * SEL_BLOCK), mask)
        p = p.reshape(B, G, Q_BLOCK, HPG, n_sel, SEL_BLOCK).astype(vg.dtype)
        return jnp.einsum('bgqhnk,bgqnkd->bqghd', p, vg)

    o_s = lax.map(sel_step, (q_blk, idx_blk, jnp.arange(n_q)))
    o_s = jnp.moveaxis(o_s, 0, 1).reshape(B, S, NSA_HEADS, DH)

    kw_pad = jnp.pad(k_w, ((0, 0), (WINDOW, 0), (0, 0), (0, 0)))
    vw_pad = jnp.pad(v_w, ((0, 0), (WINDOW, 0), (0, 0), (0, 0)))

    def win_step(args):
        qb, i = args
        start = i * Q_BLOCK
        kb = lax.dynamic_slice_in_dim(kw_pad, start, WINDOW + Q_BLOCK, axis=1)
        vb = lax.dynamic_slice_in_dim(vw_pad, start, WINDOW + Q_BLOCK, axis=1)
        kpos = start - WINDOW + jnp.arange(WINDOW + Q_BLOCK)
        tq = start + jnp.arange(Q_BLOCK)
        mask = (kpos[None, :] <= tq[:, None]) & (kpos[None, :] > tq[:, None] - WINDOW) & (kpos[None, :] >= 0)
        lg = jnp.einsum('bqghd,bkgd->bgqhk', qb, kb) * scale
        p = masked_softmax(lg, mask[:, None, :]).astype(vb.dtype)
        return jnp.einsum('bgqhk,bkgd->bqghd', p, vb)

    o_w = lax.map(win_step, (q_blk, jnp.arange(n_q)))
    o_w = jnp.moveaxis(o_w, 0, 1).reshape(B, S, NSA_HEADS, DH)

    g = jax.nn.sigmoid(gate_logits.reshape(B, S, NSA_HEADS, 3)).astype(q.dtype)
    o = g[..., 0:1] * o_c + g[..., 1:2] * o_s + g[..., 2:3] * o_w
    return o.reshape(B, S, NSA_HEADS * DH)

def fox_mixer(q, k, v, f_logit, f_bias):
    B, S = q.shape[:2]
    H, DH = FOX_HEADS, HEAD_DIM
    scale = DH ** -0.5
    n_q = S // Q_BLOCK
    q, k, v = [a.reshape(B, S, H, DH) for a in (q, k, v)]
    log_f = jax.nn.log_sigmoid(f_logit.astype(jnp.float32) + f_bias.astype(jnp.float32))
    c = lax.cumsum(log_f, axis=1).transpose(0, 2, 1)
    q_blk = jnp.moveaxis(q.reshape(B, n_q, Q_BLOCK, H, DH), 1, 0)
    c_blk = jnp.moveaxis(c.reshape(B, H, n_q, Q_BLOCK), 2, 0)
    kpos = jnp.arange(S)

    def step(args):
        qb, cq, i = args
        tq = i * Q_BLOCK + jnp.arange(Q_BLOCK)
        lg = jnp.einsum('bqhd,bshd->bhqs', qb, k).astype(jnp.float32) * scale + (cq[..., None] - c[:, :, None, :])
        p = masked_softmax(lg, kpos[None, :] <= tq[:, None]).astype(v.dtype)
        return jnp.einsum('bhqs,bshd->bqhd', p, v)

    o = lax.map(step, (q_blk, c_blk, jnp.arange(n_q)))
    return jnp.moveaxis(o, 0, 1).reshape(B, S, H * DH)

def moe(h, router_w, router_b, w1, b1, w2, b2):
    B, S, D = h.shape
    T = B * S
    xt = h.reshape(T, D)
    logits = (xt @ router_w + router_b).astype(jnp.float32)
    top_v, top_i = lax.top_k(logits, TOP_K)
    gate = jax.nn.softmax(top_v, axis=-1)
    A = T * TOP_K
    flat_e = top_i.reshape(A)
    flat_tok = jnp.repeat(jnp.arange(T, dtype=jnp.int32), TOP_K)
    flat_w = gate.reshape(A)
    order = jnp.argsort(flat_e, stable=True)
    se, stok, sw = flat_e[order], flat_tok[order], flat_w[order]
    counts = jnp.zeros((N_EXPERTS,), jnp.int32).at[flat_e].add(1)
    padded = (counts + MOE_BLOCK - 1) // MOE_BLOCK * MOE_BLOCK
    start = jnp.cumsum(counts) - counts
    pend = jnp.cumsum(padded)
    pstart = pend - padded
    dest = pstart[se] + jnp.arange(A, dtype=jnp.int32) - start[se]
    nb = -(-A // MOE_BLOCK) + N_EXPERTS
    buf_tok = jnp.full((nb * MOE_BLOCK,), T, jnp.int32).at[dest].set(stok)
    buf_w = jnp.zeros((nb * MOE_BLOCK,), jnp.float32).at[dest].set(sw)
    blk_e = jnp.minimum(jnp.searchsorted(pend, jnp.arange(nb, dtype=jnp.int32) * MOE_BLOCK, side='right'), N_EXPERTS - 1)
    xin = jnp.concatenate([xt, jnp.zeros((1, D), xt.dtype)], axis=0)[buf_tok].reshape(nb, MOE_BLOCK, D)

    def expert_block(args):
        xb, e = args
        hc = xb @ w1[e] + b1[e]
        gt = jnp.minimum(hc[:, :D_FF], SWIGLU_LIMIT)
        up = jnp.clip(hc[:, D_FF:], -SWIGLU_LIMIT, SWIGLU_LIMIT)
        glu = gt * jax.nn.sigmoid(SWIGLU_ALPHA * gt)
        return ((up + 1.0) * glu) @ w2[e] + b2[e]

    y = lax.map(expert_block, (xin, blk_e)).reshape(nb * MOE_BLOCK, D)
    y = y * buf_w[:, None].astype(y.dtype)
    out = jnp.zeros((T + 1, D), y.dtype).at[buf_tok].add(y)[:T]
    return out.reshape(B, S, D)

def setup_inputs(seed: int = 0) -> dict:
    key = jax.random.key(seed)
    ks = jax.random.split(key, 20)
    L, D, E, F = DEPTH, D_MODEL, N_EXPERTS, D_FF
    nrm = lambda k, shape: jax.random.normal(k, shape, jnp.float32)
    return {
        'x': nrm(ks[0], (BATCH, SEQ, D)),
        'positions': jax.random.randint(ks[1], (BATCH, 1), 0, 1024, jnp.int32) + jnp.arange(SEQ, dtype=jnp.int32)[None, :],
        'norm1_g': 1.0 + 0.02 * nrm(ks[2], (L, D)),
        'w_in': nrm(ks[3], (L, D, IN_COLS)) * D ** -0.5,
        'cmp_pos_emb': 0.1 * nrm(ks[4], (L, 2, CMP_BLOCK, HEAD_DIM)),
        'cmp_w1': nrm(ks[5], (L, 2, CMP_BLOCK * HEAD_DIM, HEAD_DIM)) * (CMP_BLOCK * HEAD_DIM) ** -0.5,
        'cmp_w2': nrm(ks[6], (L, 2, HEAD_DIM, HEAD_DIM)) * HEAD_DIM ** -0.5,
        'fox_f_bias': 2.0 + 0.5 * nrm(ks[7], (L, FOX_HEADS)),
        'w_proj_nsa': nrm(ks[8], (L, NSA_Q, D)) * NSA_Q ** -0.5,
        'w_proj_fox': nrm(ks[9], (L, FOX_W, D)) * FOX_W ** -0.5,
        'w_out': nrm(ks[10], (L, D, D)) * D ** -0.5,
        'norm2_g': 1.0 + 0.02 * nrm(ks[11], (L, D)),
        'router_w': nrm(ks[12], (L, D, E)) * D ** -0.5,
        'router_b': 0.01 * nrm(ks[13], (L, E)),
        'expert_w1': nrm(ks[14], (L, E, D, 2 * F)) * D ** -0.5,
        'expert_b1': 0.01 * nrm(ks[15], (L, E, 2 * F)),
        'expert_w2': nrm(ks[16], (L, E, F, D)) * F ** -0.5,
        'expert_b2': 0.01 * nrm(ks[17], (L, E, D)),
        'norm_f_g': 1.0 + 0.02 * nrm(ks[18], (D,)),
    }

def reference(x, positions, norm1_g, w_in, cmp_pos_emb, cmp_w1, cmp_w2, fox_f_bias, w_proj_nsa, w_proj_fox, w_out, norm2_g, router_w, router_b, expert_w1, expert_b1, expert_w2, expert_b2, norm_f_g):
    for l in range(DEPTH):
        h = rms_norm(x, norm1_g[l])
        (nq, nkc, nvc, nks, nvs, nkw, nvw, ngate, fq, fk, fv, ff, gate_nsa, gate_fox) = jnp.split(h @ w_in[l], IN_SPLITS, axis=-1)
        o_nsa = nsa_mixer(nq, nkc, nvc, nks, nvs, nkw, nvw, ngate, positions, cmp_pos_emb[l], cmp_w1[l], cmp_w2[l])
        o_fox = fox_mixer(fq, fk, fv, ff, fox_f_bias[l])
        mixed = jax.nn.sigmoid(gate_nsa) * (o_nsa @ w_proj_nsa[l]) + jax.nn.sigmoid(gate_fox) * (o_fox @ w_proj_fox[l])
        x = x + mixed @ w_out[l]
        x = x + moe(rms_norm(x, norm2_g[l]), router_w[l], router_b[l], expert_w1[l], expert_b1[l], expert_w2[l], expert_b2[l])
    return rms_norm(x, norm_f_g)


_drawn_inputs = setup_inputs


def setup_inputs(seed=0):
    import zlib

    import numpy as np

    out = dict(_drawn_inputs(seed))
    spreads = {}
    factors = {'expert_b1': 8.0, 'expert_b2': 8.0, 'norm_f_g': 2.908}
    for name, (base, spread) in spreads.items():
        noise = np.random.default_rng([zlib.crc32(name.encode()), seed]).standard_normal(out[name].shape)
        drawn = base * np.exp(spread * noise) if base else spread * noise
        out[name] = __import__('jax').numpy.asarray(drawn.astype(out[name].dtype))
    for name, factor in factors.items():
        out[name] = (out[name] * factor).astype(out[name].dtype)
    return out
```

```python
from contextlib import ExitStack

import numpy as np

import concourse.bass as bass
from concourse import mybir

F32 = mybir.dt.float32
BF16 = mybir.dt.bfloat16
I32 = mybir.dt.int32
ALU = mybir.AluOpType
ACT = mybir.ActivationFunctionType
AX = mybir.AxisListType

P = 128
S = 512
D = 1024
NT = S // P
NK = D // P
DH = 64
NH = 8
G = 2
HPG = NH // G
CB, CS = 32, 16
NC = (S - CB) // CS + 1
ROT = DH // 4
E = 32
TOPK = 4
F = D
MAX_EXTRA = (TOPK * S - 1) // (P + 1)
EPS = 1e-6
NEG = -1e30
SCALE = DH ** -0.5
ALPHA, LIMIT = 1.702, 7.0

SIZES = [NH * DH] + [G * DH] * 6 + [NH * 3] + [NH * DH] * 3 + [NH, D, D]
(C_Q, C_KC, C_VC, C_KS, C_VS, C_KW, C_VW, C_GATE, C_FQ, C_FK, C_FV, C_FF, C_GN, C_GF) = [
    int(v) for v in np.cumsum([0] + SIZES[:-1])]
N_SMALL = C_FQ - C_KC + NH
N_VW = P + NH * 3 + NH

P_OFF = {3: 0, 2: 512, 0: 896, 1: 1024}
P_LEN = 1280
PT_OFF = {0: 0, 1: 4, 3: 7, 2: 8}
PT_FILLS = [[(0, 0), (0, 1), (0, 2), (0, 3)], [(1, 1), (1, 2), (1, 3), (3, 3)], [(2, 2), (2, 3)]]

MAGIC = 1.5 * 2.0 ** 23
TWO_PI = 2 * np.pi
PI1 = 6.28125
PI2 = float(np.float32(TWO_PI - PI1) - np.float32(TWO_PI - PI1) % np.float32(2.0 ** -20))
PI3 = float(np.float32(TWO_PI - PI1 - PI2))


class Steps:

    def __init__(self, eng, sem):
        self.eng, self.sem, self.n, self.turn = eng, sem, 0, 0

    def link(self, ins):
        ins.then_inc(self.sem, 1)
        self.n += 1
        self.eng.wait_ge(self.sem, self.turn + self.n)

    def enter(self, i, per):
        self.turn, self.first, self.per = i * per, self.n, per

    def leave(self, turns):
        assert self.n - self.first == self.per, (self.n - self.first, self.per)
        self.turn, self.n = 0, self.first + turns * self.per


PAIRS = NH // 2

PRE = (["hT%d" % c for c in range(NK)] + ["kc", "vc", "ks", "kw", "vs", "vw0", "vw1", "gn0", "gf0", "ffT",
       "swks0", "swks1", "swkw0", "swkw1", "gn1", "gf1", "hk", "hv", "gn2", "gf2", "kcmp", "vcmp", "q",
       "gn3", "gf3", "swq0", "swq1"])
NSA_BODY = ["cmp", "gn", "q", "pc0", "pc1", "gf", "swq0", "swq1"]
NSA_LAST = ["cmp", "gn", "pc0", "pc1", "gf"]
GATES_PRE = NK - PAIRS
FOX_BODY = ["fq", "fk", "fv0", "fv1"]
BANKS = 8
O_BANK, WORK = 6, 7


class Fills:

    def __init__(self, start, names, i=0):
        self.at = {n: start + k for k, n in enumerate(names)}
        self.i, self.per = i, len(names)

    def __call__(self, name):
        return WORK, self.at[name] + self.i * self.per


class PreFills:
    def __call__(self, name):
        n = PRE.index(name)
        return n % BANKS, n // BANKS


N_NSA = sum(n % BANKS == WORK for n in range(len(PRE)))
N_NSA_LAST = N_NSA + (PAIRS - 1) * len(NSA_BODY)
N_FOX_PRE = N_NSA_LAST + len(NSA_LAST)
N_FOX = N_FOX_PRE + len(FOX_BODY)
N_WORK = N_FOX + (PAIRS - 1) * len(FOX_BODY)

DVE_NSA = 25
DVE_FOX = 8


def hybrid_block(nc, x, positions, norm1_g, w_in, cmp_pos_emb, cmp_w1, cmp_w2, fox_f_bias, w_proj_nsa,
                 w_proj_fox, w_out, norm2_g, router_w, router_b, expert_w1, expert_b1, expert_w2,
                 expert_b2, norm_f_g, rope_freqs, out):
    with ExitStack() as ctx:
        def sb(name, shape, dt=F32):
            return ctx.enter_context(nc.sbuf_tensor(name, shape, dt))

        def sem(name):
            return ctx.enter_context(nc.semaphore(name))

        x_v = x[0].rearrange("(t p) d -> p t d", p=P)
        w_in_v = w_in[0].rearrange("(c p) n -> p c n", p=P)
        w_out_v = w_out[0].rearrange("(c p) n -> p c n", p=P)
        out_v = out[0].rearrange("(t p) d -> p t d", p=P)
        decay_d = nc.dram_tensor("decay", (2, NH, S), F32, kind="Internal").ap()

        ring = sb("ring", [P, 12, 2048])
        stage = ring[:, 6:12, :].rearrange("p a b -> p (a b)")

        ring_f = ring[:, 0:6, :].rearrange("p a b -> p (a b)")
        w_gate = [[ring_f[:, 1024 * (2 * b + n):1024 * (2 * b + n + 1)].rearrange("p (c n) -> p c n", c=NK)
                   for n in range(2)] for b in range(2)]
        gate_raw = ring_f[:, 4096:4096 + NK * 2 * S].rearrange("p (c n s) -> p c n s", c=NK, n=2)

        def staged(at, *dims):
            n = int(np.prod(dims))
            v = stage[:, at:at + n]
            return v.rearrange("p (a b) -> p a b", a=dims[0]) if len(dims) == 2 else v.rearrange(
                "p (a b c) -> p a b c", a=dims[0], b=dims[1])

        w_small = staged(0, NK, N_SMALL)
        o1 = NK * N_SMALL
        w_q = staged(o1, NK, P)
        o2 = o1 + NK * P
        w_c1 = staged(o2, 2, 16, DH)
        w_c2 = staged(o2 + 2 * 16 * DH, 2, DH)
        pos_c = staged(o2 + 2 * 16 * DH + 2 * DH, 2, 16)
        w_fox = staged(0, 3, NK, P)

        xs = sb("xs", [P, NT, D])
        hT = sb("hT", [P, NK, S])
        mixT = sb("mixT", [P, NK, S])
        mix_f = mixT[:, :, :].rearrange("p a b -> p (a b)")
        probs = mix_f[:, 0:2 * P_LEN].rearrange("p (a b) -> p a b", a=2)
        ropeT = mix_f[0:DH, 2 * P_LEN:2 * P_LEN + 2 * S].rearrange("p (a b) -> p a b", a=2)
        xn = mix_f.rearrange("p (t d) -> p t d", t=NT)
        oT_nsa = sb("oT_nsa", [P, PAIRS, S])
        oT_fox = sb("oT_fox", [P, PAIRS, S])
        kT_sel_all = sb("kT_sel", [P, G, S])
        kT_win_all = sb("kT_win", [P, G, S])
        kT_sel, kT_win = kT_sel_all[0:DH, :, :], kT_win_all[0:DH, :, :]
        v_sel = sb("v_sel", [P, NT, P])
        v_win = sb("v_win", [P, NT, P])
        qk = sb("qk", [P, 4, S])
        q_plain, q_rope = qk[0:DH, 0:2, :], qk[0:DH, 2:4, :]
        q_fox, k_fox = qk[0:DH + 2, 0:2, :], qk[0:DH + 2, 2:4, :]
        v_fox = sb("v_fox", [P, NT, P])
        pT = sb("pT", [P, 2, P_LEN])
        pT_f = pT[:, :, :].rearrange("p a b -> p (a b)")
        kv_c = pT_f[:, 0:4 * S].rearrange("p (k g s) -> p k g s", k=2, g=G)
        pcT = sb("pcT", [DH, 2, S])
        pc = sb("pc", [P, 2, NT, NC])
        mask = sb("mask", [P, S])
        cmp_neg = sb("cmp_neg", [P, 2, NT, NC])
        cmp_one = sb("cmp_one", [P, 2, NT, NC])
        rope_cos = sb("rope_cos", [DH, S])
        rope_sin = sb("rope_sin", [DH, S])
        ident = sb("ident", [P, P])
        swap = sb("swap", [DH, DH])
        kT_cmp = sb("kT_cmp", [DH, G, NC])
        v_cmp = sb("v_cmp", [NC, G, DH])
        gates = sb("gates", [P, NH * 3, NT])
        g1 = sb("g1", [P, NK])
        f_bias = sb("f_bias", [P, NH])
        st = sb("st", [P, 64])
        ss1, rs1, tmp1, tmp2 = st[:, 0:4], st[:, 4:8], st[:, 8:12], st[:, 12:16]
        mx, ngm, sums, wts = (st[:, 16 + 8 * k:24 + 8 * k].rearrange("p (a b) -> p a b", a=2) for k in range(4))
        cmx, csum = st[:, 48:56].rearrange("p (a b) -> p a b", a=2), st[:, 56:64].rearrange("p (a b) -> p a b", a=2)
        lf = sb("lf", [P, 3, NT, NH])
        ones8, decay = oT_fox[0:NH, 0, :], oT_fox[0:NH, 1:3, :]
        pos_i = oT_fox[0:DH, 3, :].bitcast(I32)
        hid = pcT[:, :, :].rearrange("p a s -> p (a s)")[:, 0:3 * 2 * G * NC].rearrange(
            "p (m k g c) -> p m k g c", m=3, k=2, g=G)
        hbias = sb("hbias", [DH, 2])
        freq = sb("freq", [DH, 1])
        ang = oT_nsa[0:DH, :, :]

        ps = ctx.enter_context(nc.psum_tensor("ps", [P, 8, 512], F32))
        o_bank = ps[:, O_BANK, :]

        def work(b):
            return ps[:, b, :]

        def scores(h, t):
            bank, at = {3: (0, 0), 2: (1, 0), 0: (1, 384), 1: (2, 0)}[t]
            return ps[:, 3 * h + bank, at:at + P * (t + 1)]

        x_loaded = [sem("x_loaded%d" % t) for t in range(NT)]
        small_loaded = sem("small_loaded")
        pos_loaded = sem("pos_loaded")
        w_small_loaded = sem("w_small_loaded")
        w_cmp_loaded = sem("w_cmp_loaded")
        w_q_loaded = sem("w_q_loaded")
        w_gate_loaded = [sem("w_gate_loaded%d" % b) for b in range(2)]
        w_fqk_loaded = sem("w_fqk_loaded")
        w_fv_loaded = sem("w_fv_loaded")
        decay_stored = sem("decay_stored")
        decay_rows = sem("decay_rows")
        consts = sem("consts")
        act_step = sem("act_step")
        dve_step = sem("dve_step")
        pool_step = sem("pool_step")
        pe_took, pool_took, dve_took = sem("pe_took"), sem("pool_took"), sem("dve_took")
        squares = sem("squares")
        root = sem("root")
        mean_sq = sem("mean_sq")
        x_normed = sem("x_normed")
        work_full = [sem("work_full%d" % b) for b in range(BANKS)]
        work_free = [sem("work_free%d" % b) for b in range(BANKS)]
        angles = sem("angles")
        sines = sem("sines")
        raw_k_ready = sem("raw_k_ready")
        pool_rope = sem("pool_rope")
        rope_done = sem("rope_done")
        lf_abs = sem("lf_abs")
        lf_ln = sem("lf_ln")
        lf_ready = sem("lf_ready")
        decay_ready = sem("decay_ready")
        hid_in = sem("hid_in")
        hid_tanh = sem("hid_tanh")
        hid_ready = sem("hid_ready")
        cmp_ready = sem("cmp_ready")
        q_ready = sem("q_ready")
        scores_ready = sem("scores_ready")
        half_free = sem("half_free")
        max_ready = sem("max_ready")
        probs_ready = sem("probs_ready")
        turned_ready = sem("turned_ready")
        weights_ready = sem("weights_ready")
        normed = sem("normed")
        pT_ready = sem("pT_ready")
        pT_free = sem("pT_free")
        cmp_shifted = sem("cmp_shifted")
        cmp_exp = sem("cmp_exp")
        cmp_weighted = sem("cmp_weighted")
        cmp_masked = sem("cmp_masked")
        pcT_ready = sem("pcT_ready")
        pcT_used = sem("pcT_used")
        o_free = sem("o_free")
        fox_qk_ready = sem("fox_qk_ready")
        fox_v_ready = sem("fox_v_ready")

        slots_d = nc.dram_tensor("slots", (E * S, 1), F32, kind="Internal").ap()
        table_d = nc.dram_tensor("table", (S + 1, D), F32, kind="Internal").ap()
        y_d = nc.dram_tensor("y", (TOPK * S, D), F32, kind="Internal").ap()
        NOWHERE = TOPK * S

        w_mix = [{"pn": staged(3072 * (b + 1) + 2048, PAIRS, P), "pf": staged(3072 * (b + 1) + 2560, PAIRS, P)}
                 for b in range(2)]
        w_o = [stage[:, at:at + D] for at in (9728, 10752, 0, 1024, 2048, 3072, 4096, 5120)]
        b_raw = staged(6144, 1, 3 * D)[0:E, 0, :]
        b_mid = oT_nsa[:, :, :].rearrange("p a s -> p (a s)")[0:E, 0:3 * D // 2].bitcast(BF16)
        qk_f = qk[:, :, :].rearrange("p a s -> p (a s)")
        gate_sig = [qk[:, 2 * b:2 * b + 2, :] for b in range(2)]
        bias = qk_f[0:3 * E, 0:3 * D // 2].bitcast(BF16)
        pick = pT_f[0:3 * E, 0:E * P // 2].bitcast(BF16).rearrange("p (e m) -> p e m", e=E)
        xn2 = hT[:, :, :].rearrange("p a s -> p (a s)").rearrange("p (t d) -> p t d", t=NT)
        h2T = mixT
        w_r = v_sel[:, :, :].rearrange("p a b -> p (a b)")[:, 0:NK * E].rearrange("p (c e) -> p c e", c=NK)
        rt = [kk[:, g, :].rearrange("p (a t e) -> p a t e", a=4, t=NT) for kk in (kT_sel_all, kT_win_all) for g in range(G)]
        logit, over, tied, run, chosen, expd, rank, dest = (rt[n // 4][:, n % 4] for n in range(8))
        hot, prod, upto = (rt[2][:, n] for n in range(3))
        r_bias, e_base, one_e = (rt[3][:, 0, n, :] for n in range(3))
        cum, many, one_row = (rt[3][:, 1, n, :] for n in range(3))
        earlier = v_win[:, 0, :]
        ones = v_win[:, 1, :]
        small2 = v_win[:, 2, :]
        top8 = small2[:, 0:32].rearrange("p (t m) -> p t m", t=NT)
        dest_k, gate_k = (small2[:, 32 + 16 * n:48 + 16 * n].rearrange("p (k t) -> p k t", k=TOPK) for n in range(2))
        dest_i = small2[:, 64:80].bitcast(I32).rearrange("p (k t) -> p k t", k=TOPK)
        slot_val = small2[:, 80:96].rearrange("p (t k) -> p t k", t=NT)
        ss2, rs2, tmp3, tmp4, n_over, r_sum = (small2[:, 96 + 4 * n:100 + 4 * n] for n in range(6))
        g2 = small2[:, 120:128]
        idx = v_win[:, 3, :].bitcast(I32)
        idx_y, idx_x = idx[:, 0:E], idx[:, E:2 * E]
        now_x, now_y = ([idx[:, 2 * E + 2 * n + b:2 * E + 2 * n + b + 1] for b in range(2)] for n in range(2))
        over_f = v_win[:, 3, 72:73]
        extra = idx[0:1, 80:128]
        slots_sb = v_fox[0:E, 0, :]
        fill_sb = v_fox[:, 1, :]
        zero_sb = pcT[0:1, :, :].rearrange("p a s -> p (a s)")
        ov = [rope_cos[0:1, :].rearrange("p (o e) -> p o e", o=16), rope_sin[0:1, :].rearrange("p (o e) -> p o e", o=16)]
        ov_o, ov_e, ov_s = (cmp_neg[0:1, :, :, :].rearrange("p a b c -> p (a b c)")[:, 16 * n:16 * n + 16] for n in range(3))

        def halves(v):
            return [v[:, 1024 * n:1024 * n + 1024] for n in range(v.shape[1] // 1024)]

        oTn_f = oT_nsa[:, :, :].rearrange("p a s -> p (a s)")
        oTf_f = oT_fox[:, :, :].rearrange("p a s -> p (a s)")
        hT_f = hT[:, :, :].rearrange("p a s -> p (a s)")
        xg = halves(oTn_f)
        xT = [v.rearrange("p (c m) -> p c m", c=NK) for v in halves(oTf_f)]
        gT = [v.rearrange("p (c m) -> p c m", c=NK) for v in halves(hT_f[:, 0:2048])]
        yb = halves(hT_f[:, 2048:4096])
        gt_b, up_b, sg_b, act_b = halves(mix_f)
        y_in = [ring[:, 2 * t:2 * t + 2, :].rearrange("p a b -> p (a b)").rearrange("p (k d) -> p k d", k=TOPK)
                for t in range(NT)]
        gf_b = oTn_f[:, 0:1024]

        hc_g = ps[:, 0:2, :].rearrange("p a b -> p (a b)")
        hc_u = ps[:, 2:4, :].rearrange("p a b -> p (a b)")
        y_ps = ps[:, 4:6, :].rearrange("p a b -> p (a b)")

        w_mix_loaded = [sem("w_mix_loaded%d" % b) for b in range(2)]
        w_o_loaded = sem("w_o_loaded")
        b_loaded = sem("b_loaded")
        router_loaded = sem("router_loaded")
        mix_full = sem("mix_full")
        mix_sig = sem("mix_sig")
        mix_free = sem("mix_free")
        mix_used = sem("mix_used")
        out_full = sem("out_full")
        x2_ready = sem("x2_ready")
        xn2_ready = sem("xn2_ready")
        h2T_full = sem("h2T_full")
        h2T_ready = sem("h2T_ready")
        logits_full = sem("logits_full")
        chosen_ready = sem("chosen_ready")
        shifted = sem("shifted")
        expd_ready = sem("expd_ready")
        pos_full = sem("pos_full")
        dest_ready = sem("dest_ready")
        bias_hi = sem("bias_hi")
        bias_rest = sem("bias_rest")
        bias_ready = sem("bias_ready")
        consts2 = sem("consts2")
        table_stored = sem("table_stored")
        slots_filled = sem("slots_filled")
        slots_stored = sem("slots_stored")
        slots_loaded = sem("slots_loaded")
        slots_turned = sem("slots_turned")
        idx_ready = sem("idx_ready")
        slab_loaded = [sem("slab_loaded%d" % b) for b in range(12)]
        w1_used = sem("w1_used")
        w2_used = sem("w2_used")
        now_ready = sem("now_ready")
        xg_loaded = [sem("xg_loaded%d" % b) for b in range(2)]
        xT_full = sem("xT_full")
        xT_ready = sem("xT_ready")
        gt_ready = sem("gt_ready")
        hc_free = sem("hc_free")
        sg_ready = sem("sg_ready")
        act_ready = sem("act_ready")
        gT_full = sem("gT_full")
        gT_ready = sem("gT_ready")
        y_ready = sem("y_ready")
        y_stored = [sem("y_stored%d" % b) for b in range(2)]
        extra_ready = sem("extra_ready")
        ov_idx = sem("ov_idx")
        ov_now = sem("ov_now")
        ov_w = sem("ov_w")
        ov_xg = sem("ov_xg")
        ov_pe = sem("ov_pe")
        ov_dve = sem("ov_dve")
        ov_act = sem("ov_act")
        ov_y = sem("ov_y")
        y_loaded = [sem("y_loaded%d" % t) for t in range(NT)]
        gf_loaded = sem("gf_loaded")
        sum_ready = sem("sum_ready")
        result = sem("result")
        stored = sem("stored")
        sp_took = sem("sp_took")
        ov_over = sem("ov_over")
        ov_part = sem("ov_part")
        ov_done = sem("ov_done")
        glu_ready = sem("glu_ready")
        now_y_ready = sem("now_y_ready")

        block = ctx.enter_context(nc.Block())

        @block.sync
        def _(sp):
            for t in range(NT):
                sp.dma_start(xs[:, t, :], x_v[:, t, :]).then_inc(x_loaded[t], 16)
            sp.dma_start(g1[:, :], norm1_g[0].rearrange("(c p) -> p c", p=P), allow_slow_non_contiguous=True).then_inc(small_loaded, 16)
            sp.dma_start(f_bias[:, :], fox_f_bias[0:1, :].partition_broadcast(P)).then_inc(small_loaded, 16)
            sp.dma_start(freq[:, :], rope_freqs[:, :]).then_inc(pos_loaded, 16)
            sp.dma_start(pos_i, positions[0:1, :].partition_broadcast(DH)).then_inc(pos_loaded, 16)
            sp.dma_start(w_small[:, :, 0:C_FQ - C_KC], w_in_v[:, :, C_KC:C_FQ]).then_inc(w_small_loaded, 16)
            sp.dma_start(w_small[:, :, C_FQ - C_KC:], w_in_v[:, :, C_FF:C_GN]).then_inc(w_small_loaded, 16)
            for j in range(2):
                sp.dma_start(w_c1[:, j, :, :], cmp_w1[0, j].rearrange("(l p) h -> p l h", p=P)).then_inc(w_cmp_loaded, 16)
                sp.dma_start(w_c2[0:DH, j, :], cmp_w2[0, j]).then_inc(w_cmp_loaded, 16)
                sp.dma_start(pos_c[:, j, :], cmp_pos_emb[0, j].rearrange("(l two) d -> (two d) l", two=2),
                             allow_slow_non_contiguous=True)\
                  .then_inc(w_cmp_loaded, 16)

            def load_q(i):
                for a in range(G):
                    sp.dma_start(w_q[:, :, a * DH:(a + 1) * DH],
                                 w_in_v[:, :, bass.ds(C_Q + a * HPG * DH + i * DH, DH)]).then_inc(w_q_loaded, 16)

            def load_gate(c, b):
                for n, at in enumerate((C_GN, C_GF)):
                    sp.dma_start(w_gate[b][n], w_in_v[:, :, bass.ds(at + P * c, P)]).then_inc(w_gate_loaded[b], 16)

            load_gate(0, 0)
            load_q(0)
            load_gate(1, 1)
            for c in range(2, GATES_PRE + 1):
                b, n = PreFills()("gf%d" % (c - 2))
                sp.wait_ge(work_full[b], n + 1)
                load_gate(c, c % 2)
            b, n = PreFills()("q")
            sp.wait_ge(work_full[b], n + 1)
            load_q(1)
            with sp.Fori(0, PAIRS - 2) as i:
                b, n = Fills(N_NSA, NSA_BODY, i)("q")
                sp.wait_ge(work_full[b], n + 1)
                load_q(i + 2)
                b, n = Fills(N_NSA, NSA_BODY, i)("gf")
                sp.wait_ge(work_full[b], n + 1)
                load_gate(i + GATES_PRE + 1, 0)

            def load_fox(j, part):
                at = (C_FQ, C_FK, C_FV)[part]
                sp.dma_start(w_fox[:, part, :, :], w_in_v[:, :, bass.ds(at + P * j, P)])\
                  .then_inc(w_fv_loaded if part == 2 else w_fqk_loaded, 16)

            def load_decay(j):
                sp.dma_start(q_fox[DH:DH + 1, :, :], decay_d[0:1, bass.ds(2 * j, 2), :]).then_inc(decay_rows, 16)
                sp.dma_start(k_fox[DH + 1:DH + 2, :, :], decay_d[1:2, bass.ds(2 * j, 2), :]).then_inc(decay_rows, 16)

            b, n = PreFills()("vcmp")
            sp.wait_ge(work_full[b], n + 1)
            for part in range(3):
                load_fox(0, part)
            sp.wait_ge(decay_ready, 1)
            sp.dma_start(decay_d[0], decay[:, 0, :]).then_inc(decay_stored, 16)
            sp.dma_start(decay_d[1], decay[:, 1, :]).then_inc(decay_stored, 16)
            sp.wait_ge(decay_stored, 32)
            sp.wait_ge(consts, 7)
            load_decay(0)
            b, n = Fills(N_NSA, NSA_BODY, PAIRS - 2)("gf")
            sp.wait_ge(work_full[b], n + 1)
            load_gate(NK - 1, 0)
            b, n = Fills(N_FOX_PRE, FOX_BODY)("fk")
            sp.wait_ge(work_full[b], n + 1)
            for part in range(2):
                load_fox(1, part)
            b, n = Fills(N_FOX_PRE, FOX_BODY)("fv1")
            sp.wait_ge(work_full[b], n + 1)
            load_fox(1, 2)
            with sp.Fori(0, PAIRS - 2) as j:
                b, n = Fills(N_FOX, FOX_BODY, j)("fk")
                sp.wait_ge(work_full[b], n + 1)
                load_decay(j + 1)
                for part in range(2):
                    load_fox(j + 2, part)
                b, n = Fills(N_FOX, FOX_BODY, j)("fv1")
                sp.wait_ge(work_full[b], n + 1)
                load_fox(j + 2, 2)
            b, n = Fills(N_FOX, FOX_BODY, PAIRS - 2)("fk")
            sp.wait_ge(work_full[b], n + 1)
            load_decay(PAIRS - 1)
            sp.wait_ge(decay_rows, 32 * PAIRS)

            def load_mix(c, b):
                w, s = w_mix[b], w_mix_loaded[b]
                for a in range(G):
                    src = w_proj_nsa[0].rearrange("(a i d) n -> a d i n", a=G, d=DH)[a]
                    sp.dma_start(w["pn"][a * DH:(a + 1) * DH, :, :], src[:, :, bass.ds(P * c, P)]).then_inc(s, 16)
                src = w_proj_fox[0].rearrange("(k p) n -> p k n", p=P)
                sp.dma_start(w["pf"][:, :, :], src[:, :, bass.ds(P * c, P)]).then_inc(s, 16)

            for b in range(2):
                load_mix(b, b)
            sp.dma_start(w_r, router_w[0].rearrange("(c p) e -> p c e", p=P)).then_inc(router_loaded, 16)
            for k in range(2):
                sp.dma_start(w_o[k], w_out_v[:, k, :]).then_inc(w_o_loaded, 16)
            with sp.Fori(0, NK // 2 - 1) as i:
                for b in range(2):
                    sp.wait_ge(mix_full, 2 * i + b + 1)
                    load_mix(2 * i + b + 2, b)
            sp.wait_ge(mix_full, NK - 1)
            for k in range(2, 7):
                sp.dma_start(w_o[k], w_out_v[:, k, :]).then_inc(w_o_loaded, 16)
            sp.wait_ge(mix_full, NK)
            sp.dma_start(w_o[7], w_out_v[:, 7, :]).then_inc(w_o_loaded, 16)
            sp.dma_start(b_raw[:, 0:2 * F], expert_b1[0]).then_inc(b_loaded, 16)
            sp.dma_start(b_raw[:, 2 * F:], expert_b2[0]).then_inc(b_loaded, 16)
            sp.wait_ge(consts2, 6)
            sp.dma_start(r_bias, router_b[0:1, :].partition_broadcast(P)).then_inc(router_loaded, 16)
            sp.dma_start(g2, norm2_g[0].rearrange("(c p) -> p c", p=P), allow_slow_non_contiguous=True)\
              .then_inc(router_loaded, 16)
            sp.dma_start(table_d[S:S + 1, :], zero_sb).then_inc(table_stored, 16)
            sp.dma_start(slots_d.rearrange("(a b) c -> a (b c)", a=P), fill_sb).then_inc(slots_filled, 16)

            def load_slab(e, c):
                if c < NK:
                    src = expert_w1[0].rearrange("e (c p) n -> e p c n", p=P)
                    src = src[bass.ds(e, 1), :, c, :] if not isinstance(e, int) else src[e:e + 1, :, c, :]
                    src = src.rearrange("e p n -> (e p) n")
                    dst = ring[:, c, :]
                else:
                    src = expert_w2[0].rearrange("e (s k p) n -> e p s k n", p=P, k=2)
                    src = src[bass.ds(e, 1), :, c - NK, :, :] if not isinstance(e, int) else src[e:e + 1, :, c - NK, :, :]
                    src = src.rearrange("e p k n -> (e p) k n")
                    dst = ring[:, c, :].rearrange("p (k n) -> p k n", k=2)
                sp.dma_start(dst, src).then_inc(slab_loaded[c], 16)

            sp.wait_ge(mix_sig, NK)
            for c in range(6):
                load_slab(0, c)
            sp.wait_ge(bias_ready, 2)
            sp.wait_ge(out_full, 2 * NT)
            for c in range(6, 12):
                load_slab(0, c)
            sp.wait_ge(xn2_ready, NT)
            sp.dma_start(table_d[0:S, :].rearrange("(t p) d -> p t d", p=P), xn2).then_inc(table_stored, 16)
            sp.wait_ge(slots_stored, 16 * NT * TOPK)
            sp.dma_start(slots_sb, slots_d.rearrange("(e s) c -> e (s c)", e=E)[:, 0:P]).then_inc(slots_loaded, 16)

            def load_w1(e):
                for c in range(NK):
                    sp.wait_ge(w1_used, NK * (e - 1) + c + 1)
                    load_slab(e, c)

            def load_w2(e):
                for s in range(4):
                    sp.wait_ge(w2_used, 4 * (e - 1) + s + 1)
                    load_slab(e, NK + s)

            load_w1(1)
            with sp.Fori(1, E - 1) as e:
                load_w1(e + 1)
                load_w2(e)
            load_w2(E - 1)

            sp.wait_ge(extra_ready, 1)
            sp.wait_ge(w2_used, 4 * E)
            total = sp.value_load(extra[0:1, 32:33], min_val=0, max_val=MAX_EXTRA)
            with sp.Fori(0, MAX_EXTRA) as o:
                with sp.If(total > o):
                    e = sp.value_load(extra[0:1, bass.ds(o, 1)], min_val=0, max_val=E - 1)
                    first = sp.value_load(extra[0:1, bass.ds(o + 16, 1)], min_val=0, max_val=E * S - P)
                    sp.wait_ge(ov_act, 2 * o + 2)
                    sp.sem_inc(sp_took, 1)
                    sp.dma_start(over_f, slots_d[bass.ds(first, P), :]).then_inc(ov_idx, 16)
                    for c in range(NK):
                        src = expert_w1[0].rearrange("e (c p) n -> e p c n", p=P)[bass.ds(e, 1), :, c, :]
                        sp.dma_start(ring[:, c, :], src.rearrange("e p n -> (e p) n")).then_inc(ov_w, 16)
                    for c in range(4):
                        src = expert_w2[0].rearrange("e (s k p) n -> e p s k n", p=P, k=2)[bass.ds(e, 1), :, c, :, :]
                        sp.dma_start(ring[:, NK + c, :].rearrange("p (k n) -> p k n", k=2),
                                     src.rearrange("e p k n -> (e p) k n")).then_inc(ov_w, 16)

            sp.wait_ge(ov_done, 1)
            for t in range(NT):
                sp.dma_start(y_in[t], y_d.rearrange("(t p k) d -> t p k d", p=P, k=TOPK)[t]).then_inc(y_loaded[t], 16)
                if t == 0:
                    sp.dma_start(gf_b, norm_f_g.unsqueeze(0).partition_broadcast(P)).then_inc(gf_loaded, 16)
            for t in range(NT):
                sp.wait_ge(result, t + 1)
                sp.dma_start(out_v[:, t, :], y_in[t][:, 0, :]).then_inc(stored, 16)
            sp.wait_ge(stored, 16 * NT)

        @block.gpsimd
        def _(pool):
            step = Steps(pool, pool_step)

            def take(semaphore, value):
                pool.wait_ge(semaphore, value)
                pool.sem_inc(pool_took, 1)

            step.link(pool.memset(ident[:, :], 0.0))
            pool.affine_select(out=ident[:, :], in_=ident[:, :], compare_op=ALU.not_equal, fill=1.0, base=0,
                               pattern=[[-1, P]], channel_multiplier=1).then_inc(consts, 1)
            step.link(pool.memset(mask[:, :], 0.0))
            tri = mask[:, S - P:S]
            pool.affine_select(out=tri, in_=tri, compare_op=ALU.is_ge, fill=NEG, base=0,
                               pattern=[[-1, P]], channel_multiplier=1).then_inc(consts, 1)
            step.link(pool.memset(swap[:, :], 0.0))
            half = ROT // 2
            step.link(pool.affine_select(out=swap[:, 0:half], in_=swap[:, 0:half], compare_op=ALU.not_equal, fill=-1.0,
                                         base=-half, pattern=[[-1, half]], channel_multiplier=1))
            pool.affine_select(out=swap[:, half:ROT], in_=swap[:, half:ROT], compare_op=ALU.not_equal, fill=1.0,
                               base=0, pattern=[[-1, half]], channel_multiplier=1).then_inc(consts, 1)
            step.link(pool.memset(cmp_neg[:, :, :, :], 0.0))
            step.link(pool.memset(cmp_one[:, :, :, :], 1.0))
            for m, fill in ((cmp_neg, NEG), (cmp_one, 0.0)):
                pool.affine_select(out=m[:, :, :, :], in_=m[:, :, :, :], compare_op=ALU.is_ge, fill=fill, base=1 - CB,
                                   pattern=[[0, 2], [P, NT], [-CS, NC]], channel_multiplier=1).then_inc(consts, 1)
            pool.memset(ones8, 1.0).then_inc(consts, 1)

            def rope_part(src):
                pool.tensor_tensor(ropeT, src, rope_cos[:, :].unsqueeze(1).broadcast_to([DH, G, S]), ALU.mult)\
                    .then_inc(pool_rope, 1)

            pool.wait_ge(consts, 6)
            pool.memset(qk[DH:DH + 2, :, :], 1.0).then_inc(consts, 1)
            pool.wait_ge(sines, 2)
            for n, src in enumerate((q_plain, q_rope)):
                pool.wait_ge(raw_k_ready, n + 1)
                if n:
                    pool.wait_ge(rope_done, n)
                rope_part(src)
            pool.wait_ge(q_ready, 1)
            pool.wait_ge(rope_done, 2)
            rope_part(q_plain)

            def nsa(i, last):
                take(cmp_weighted, i + 1)
                pool.tensor_tensor(pc[:, :, :, :], pc[:, :, :, :], cmp_one[:, :, :, :], ALU.mult).then_inc(cmp_masked, 1)
                if not last:
                    take(rope_done, i + 3)
                    take(q_ready, i + 2)
                    rope_part(q_plain)

            with pool.Fori(0, PAIRS - 1) as i:
                nsa(i, False)
            nsa(PAIRS - 1, True)

            pool.wait_ge(mix_used, 1)
            step.link(pool.memset(fill_sb, float(NOWHERE)))
            step.link(pool.memset(zero_sb, 0.0))
            step.link(pool.memset(v_win[:, 0:2, :], 1.0))
            step.link(pool.affine_select(out=earlier, in_=earlier, compare_op=ALU.is_gt, fill=0.0, base=0,
                                         pattern=[[1, P]], channel_multiplier=-1))
            pool.iota(slot_val, pattern=[[TOPK * P, NT], [1, TOPK]], base=0, channel_multiplier=TOPK,
                      allow_small_or_imprecise_dtypes=True).then_inc(consts2, 1)
            pool.iota(e_base, pattern=[[S, E]], base=0, channel_multiplier=0,
                      allow_small_or_imprecise_dtypes=True).then_inc(consts2, 1)
            pool.iota(ov_o, pattern=[[1, 16]], base=0, channel_multiplier=0,
                      allow_small_or_imprecise_dtypes=True).then_inc(consts2, 1)
            pool.memset(one_e, 1.0).then_inc(consts2, 1)
            pool.memset(one_row, 1.0).then_inc(consts2, 1)
            pool.wait_ge(consts2, 5)
            pool.memset(pick, 1.0).then_inc(consts2, 1)
            for j in range(3):
                part = pick[E * j:E * (j + 1), :, :]
                pool.wait_ge(consts2, 6 + j)
                pool.affine_select(out=part, in_=part, compare_op=ALU.is_equal, fill=0.0, base=0,
                                   pattern=[[-1, E], [0, P]], channel_multiplier=1).then_inc(consts2, 1)
            pool.wait_ge(slots_filled, 16)
            pool.wait_ge(consts2, 9)
            for k in range(TOPK):
                pool.wait_ge(dest_ready, k + 1)
                for t in range(NT):
                    pool.indirect_dma_start(out=slots_d, out_offset=bass.IndirectOffsetOnAxis(
                        ap=dest_i[:, k, t:t + 1], axis=0), in_=slot_val[:, t, k:k + 1], in_offset=None)\
                        .then_inc(slots_stored, 16)
            pool.wait_ge(idx_ready, 2)
            pool.wait_ge(table_stored, 32)

            def now_gather(e, b):
                col = idx_x[:, e:e + 1] if isinstance(e, int) else idx_x[:, bass.ds(e, 1)]
                pool.tensor_copy(now_x[b], col).then_inc(now_ready, 1)

            def gathered(b):
                pool.indirect_dma_start(out=xg[b], out_offset=None, in_=table_d,
                                        in_offset=bass.IndirectOffsetOnAxis(ap=now_x[b], axis=0))\
                    .then_inc(xg_loaded[b], 16)

            def scattered(b):
                pool.indirect_dma_start(out=y_d, out_offset=bass.IndirectOffsetOnAxis(ap=now_y[b], axis=0),
                                        in_=yb[b], in_offset=None, bounds_check=NOWHERE - 1, oob_is_err=False)\
                    .then_inc(y_stored[b], 16)

            pool.wait_ge(bias_ready, 2)
            for b in range(2):
                now_gather(b, b)
                pool.wait_ge(now_ready, b + 1)
                gathered(b)

            def block(e, b, more, scatter):
                if more:
                    take(xT_full, 2 * e + 2)
                    now_gather(e + 2, b)
                    take(now_ready, e + 3)
                    gathered(b)
                if scatter:
                    o = 1 - b
                    take(y_ready, e)
                    col = idx_y[:, e - 1:e] if isinstance(e, int) else idx_y[:, bass.ds(e - 1, 1)]
                    pool.tensor_copy(now_y[o], col).then_inc(now_y_ready, 1)
                    take(now_y_ready, e)
                    scattered(o)

            block(0, 0, True, False)
            with pool.Fori(0, E // 2 - 2) as i:
                block(2 * i + 1, 1, True, True)
                block(2 * i + 2, 0, True, True)
            block(E - 3, 1, True, True)
            block(E - 2, 0, False, True)
            block(E - 1, 1, False, True)
            pool.wait_ge(y_ready, E)
            pool.tensor_copy(now_y[1], idx_y[:, E - 1:E]).then_inc(now_y_ready, 1)
            pool.wait_ge(now_y_ready, E)
            scattered(1)

            pool.wait_ge(extra_ready, 1)
            for b in range(2):
                pool.wait_ge(y_stored[b], 16 * E // 2)
            total = pool.value_load(extra[0:1, 32:33], min_val=0, max_val=MAX_EXTRA)
            pool.sem_inc(ov_over, 1)
            with pool.Fori(0, MAX_EXTRA) as o:
                with pool.If(total > o):
                    take(ov_now, 2 * o + 2)
                    pool.indirect_dma_start(out=xg[0], out_offset=None, in_=table_d,
                                            in_offset=bass.IndirectOffsetOnAxis(ap=now_x[0], axis=0)).then_inc(ov_xg, 16)
                    take(ov_act, 2 * o + 4)
                    pool.indirect_dma_start(out=y_d, out_offset=bass.IndirectOffsetOnAxis(ap=now_y[0], axis=0),
                                            in_=yb[0], in_offset=None, bounds_check=NOWHERE - 1, oob_is_err=False)\
                        .then_inc(ov_y, 16)
                    take(ov_y, 16 * o + 16)
                    pool.sem_inc(ov_over, 1)
            pool.sem_inc(ov_done, 1)

        @block.scalar
        def _(act):
            def evacuated(fills, name, ops):
                b, n = fills(name)
                act.wait_ge(work_full[b], n + 1)
                for out_ap, at, *scale in ops:
                    src = at(work(b))
                    last = act.activation(out_ap, src, ACT.Copy, scale=scale[0] if scale else 1.0)
                last.then_inc(work_free[b], 1)
                return last

            for t in range(NT):
                act.wait_ge(x_loaded[t], 16)
                act.activation(xn[:, t, :], xs[:, t, :], ACT.Square, accum_out=ss1[:, t:t + 1]).then_inc(squares, 1)
                act.wait_ge(mean_sq, t + 1)
                act.activation(tmp1[:, t:t + 1], ss1[:, t:t + 1], ACT.Sqrt).then_inc(root, 1)
            act.wait_ge(angles, 1)
            act.activation(rope_sin[:, :], ang[:, 0, :], ACT.Sin).then_inc(sines, 1)
            act.activation(rope_cos[:, :], ang[:, 1, :], ACT.Sin).then_inc(sines, 1)
            pre = PreFills()
            act.wait_ge(small_loaded, 32)
            for c in range(0, NK, 2):
                b, n = pre("hT%d" % c)
                act.wait_ge(work_full[b], n + 1)
                act.activation(hT[:, c, :], work(b), ACT.Copy, scale=g1[:, c:c + 1]).then_inc(work_free[b], 1)
            for k, name in enumerate(("kc", "vc")):
                b, n = pre(name)
                act.wait_ge(work_full[b], n + 1)
                for g in range(G):
                    src = work(b)[g * DH:(g + 1) * DH, :]
                    act.activation(kv_c[0:DH, k, g, :], src, ACT.Copy).then_inc(act_step, 1)
                    last = act.activation(kv_c[DH:P, k, g, 0:S - 1], src[:, 1:S], ACT.Copy)
                last.then_inc(work_free[b], 1)
            for name, dst in (("ks", q_plain), ("kw", q_rope)):
                b, n = pre(name)
                act.wait_ge(work_full[b], n + 1)
                act.activation(dst[:, 0, :], work(b)[0:DH, :], ACT.Copy).then_inc(act_step, 1)
                act.activation(dst[:, 1, :], work(b)[DH:P, :], ACT.Copy).then_inc(work_free[b], 1)
                act.wait_ge(work_free[b], n + 1)
                act.sem_inc(raw_k_ready, 1)
            b, n = pre("vs")
            act.wait_ge(work_full[b], n + 1)
            act.activation(v_sel[:, :, :], work(b).rearrange("p (t c) -> p t c", t=NT), ACT.Copy)\
               .then_inc(work_free[b], 1)
            for k in range(2):
                b, n = pre("vw%d" % k)
                act.wait_ge(work_full[b], n + 1)
                src, tt = work(b)[:, 0:2 * N_VW].rearrange("p (t n) -> p t n", t=2), slice(2 * k, 2 * k + 2)
                act.activation(lf[:, 0, tt, :], src[:, :, N_VW - NH:], ACT.Copy).then_inc(act_step, 1)
                act.activation(v_win[:, tt, :], src[:, :, 0:P], ACT.Copy).then_inc(act_step, 1)
                act.activation(gates[:, :, tt].rearrange("p n t -> p t n"), src[:, :, P:N_VW - NH], ACT.Sigmoid)\
                   .then_inc(work_free[b], 1)

            def take_gate(fills, c, n, name):
                b, k = fills(name)
                dst = gate_raw[:, c, n, :] if isinstance(c, int) else \
                    gate_raw[:, bass.ds(c, 1), n, :].rearrange("p a s -> p (a s)")
                act.wait_ge(work_full[b], k + 1)
                act.activation(dst, work(b), ACT.Copy).then_inc(work_free[b], 1)

            def take_gates(c):
                take_gate(pre, c, 0, "gn%d" % c)
                take_gate(pre, c, 1, "gf%d" % c)

            take_gates(0)
            act.wait_ge(lf_abs, 1)
            act.activation(lf[:, 1, :, :], lf[:, 1, :, :], ACT.Exp, scale=-1.0).then_inc(lf_ln, 1)
            act.wait_ge(lf_abs, 2)
            act.activation(lf[:, 1, :, :], lf[:, 1, :, :], ACT.Ln).then_inc(lf_ln, 1)
            take_gates(1)
            for k in range(2):
                act.wait_ge(hid_in, k + 1)
                act.activation(hid[:, 1, k, :, :], hid[:, 1, k, :, :], ACT.Tanh).then_inc(hid_tanh, 1)
            take_gates(2)

            def take_q(fills, name, dst, scale):
                b, n = fills(name)
                act.wait_ge(work_full[b], n + 1)
                act.activation(dst[0:DH, 0, :], work(b)[0:DH, :], ACT.Copy, scale=scale).then_inc(act_step, 1)
                act.activation(dst[0:DH, 1, :], work(b)[DH:P, :], ACT.Copy, scale=scale).then_inc(work_free[b], 1)
                act.wait_ge(work_free[b], n + 1)

            act.wait_ge(rope_done, 1)
            take_q(pre, "q", q_plain, SCALE)
            act.sem_inc(q_ready, 1)
            take_gates(3)

            def exps(u, h):
                act.wait_ge(max_ready, u + 1)
                for t in range(NT):
                    last = act.activation(probs[:, h, P_OFF[t]:P_OFF[t] + P * (t + 1)], scores(h, t), ACT.Exp,
                                          bias=ngm[:, h, t:t + 1], accum_out=sums[:, h, t:t + 1])
                    last.then_inc(probs_ready, 1)

            def norm(u, h):
                act.wait_ge(weights_ready, u + 1)
                for t in range(NT):
                    p = probs[:, h, P_OFF[t]:P_OFF[t] + P * (t + 1)]
                    act.activation(p, p, ACT.Copy, scale=wts[:, h, t:t + 1]).then_inc(normed, 1)

            act.sem_inc(half_free, 2)
            act.sem_inc(o_free, 1)

            def nsa(i, last):
                f = Fills(N_NSA_LAST, NSA_LAST) if last else Fills(N_NSA, NSA_BODY, i)
                act.wait_ge(cmp_shifted, i + 1)
                act.activation(pc[:, :, :, :], pc[:, :, :, :], ACT.Exp).then_inc(cmp_exp, 1)
                exps(4 * i, 0)
                exps(4 * i + 1, 1)
                norm(4 * i, 0)
                norm(4 * i + 1, 1)
                take_gate(f, GATES_PRE + i, 0, "gn")
                exps(4 * i + 2, 0)
                norm(4 * i + 2, 0)
                if not last:
                    act.wait_ge(pool_rope, i + 3)
                    take_q(f, "q", q_plain, SCALE)
                    act.sem_inc(q_ready, 1)
                exps(4 * i + 3, 1)
                take_gate(f, GATES_PRE + i, 1, "gf")
                norm(4 * i + 3, 1)
                act.wait_ge(pT_free, 2 + 4 * i + 4)
                act.activation(oT_nsa[:, i, :] if isinstance(i, int) else
                               oT_nsa[:, bass.ds(i, 1), :].rearrange("p a s -> p (a s)"), o_bank, ACT.Copy)\
                   .then_inc(o_free, 1)

            with act.Fori(0, PAIRS - 1) as i:
                nsa(i, False)
            nsa(PAIRS - 1, True)

            def fox_qk(f):
                take_q(f, "fq", q_fox, SCALE)
                take_q(f, "fk", k_fox, 1.0)
                act.sem_inc(fox_qk_ready, 1)

            fox_qk(Fills(N_FOX_PRE, FOX_BODY))

            def fox(j, last):
                exps(4 * PAIRS + 2 * j, 0)
                exps(4 * PAIRS + 2 * j + 1, 1)
                for h in range(2):
                    norm(4 * PAIRS + 2 * j + h, h)
                if not last:
                    fox_qk(Fills(N_FOX, FOX_BODY, j))
                act.wait_ge(pT_free, 2 + 4 * PAIRS + 2 * j + 2)
                act.activation(oT_fox[:, j, :] if isinstance(j, int) else
                               oT_fox[:, bass.ds(j, 1), :].rearrange("p a s -> p (a s)"), o_bank, ACT.Copy)\
                   .then_inc(o_free, 1)

            with act.Fori(0, PAIRS - 1) as j:
                fox(j, False)
            fox(PAIRS - 1, True)

            with act.Fori(0, NK // 2) as i:
                for b in range(2):
                    act.wait_ge(mix_used, 2 * i + b + 1)
                    act.activation(gate_sig[b], gate_raw[:, bass.ds(2 * i + b, 1), :, :].rearrange("p a n s -> p (a n) s"),
                                   ACT.Sigmoid).then_inc(mix_sig, 1)
            act.wait_ge(b_loaded, 32)
            act.wait_ge(mix_used, NK + 2)
            act.activation(bias[0:E, :], b_raw, ACT.Copy).then_inc(bias_hi, 1)
            act.wait_ge(bias_rest, 1)
            act.activation(b_mid, b_raw, ACT.Copy).then_inc(bias_hi, 1)
            act.wait_ge(bias_hi, 2)
            act.activation(bias[E:2 * E, :], b_mid, ACT.Copy).then_inc(bias_ready, 1)
            act.wait_ge(bias_rest, 2)
            act.activation(bias[2 * E:3 * E, :], b_raw, ACT.Copy).then_inc(bias_ready, 1)
            for t in range(NT):
                act.wait_ge(x2_ready, 2 * t + 2)
                act.activation(xn2[:, t, :], xs[:, t, :], ACT.Square, accum_out=ss2[:, t:t + 1]).then_inc(squares, 1)
            act.wait_ge(mean_sq, NT + 1)
            act.activation(tmp3, ss2, ACT.Sqrt).then_inc(root, 1)
            act.wait_ge(router_loaded, 48)
            for c in range(0, NK, 2):
                act.wait_ge(h2T_full, c + 1)
                act.activation(h2T[:, c, :], ps[:, c, :], ACT.Copy, scale=g2[:, c:c + 1]).then_inc(h2T_ready, 1)
            act.wait_ge(shifted, 1)
            act.activation(expd, expd, ACT.Exp).then_inc(expd_ready, 1)

            def sigmoid(e):
                act.wait_ge(gt_ready, e + 1)
                act.activation(sg_b, gt_b, ACT.Sigmoid, scale=ALPHA).then_inc(sg_ready, 1)

            def take_y(e, b, k):
                act.wait_ge(w2_used, 4 * e + 4)
                if not (isinstance(k, int) and k == 0):
                    act.wait_ge(y_stored[b], 16 * k)
                act.activation(yb[b], y_ps, ACT.Copy).then_inc(y_ready, 1)

            sigmoid(0)
            sigmoid(1)
            take_y(0, 0, 0)
            sigmoid(2)
            take_y(1, 1, 0)
            with act.Fori(0, (E - 4) // 2) as i:
                for b in range(2):
                    sigmoid(2 * i + b + 3)
                    take_y(2 * i + b + 2, b, i + 1)
            sigmoid(E - 1)
            take_y(E - 2, 0, E // 2 - 1)
            take_y(E - 1, 1, E // 2 - 1)

            act.wait_ge(extra_ready, 1)
            for b in range(2):
                act.wait_ge(y_stored[b], 16 * E // 2)
            total = act.value_load(extra[0:1, 32:33], min_val=0, max_val=MAX_EXTRA)
            act.sem_inc(ov_act, 2)
            with act.Fori(0, MAX_EXTRA) as o:
                with act.If(total > o):
                    act.wait_ge(ov_dve, 4 * o + 2)
                    act.activation(sg_b, gt_b, ACT.Sigmoid, scale=ALPHA).then_inc(ov_act, 1)
                    act.wait_ge(ov_pe, 4 * o + 4)
                    act.wait_ge(ov_over, o + 1)
                    act.activation(yb[0], y_ps, ACT.Copy).then_inc(ov_act, 1)
            for t in range(NT):
                act.wait_ge(sum_ready, t + 1)
                act.activation(y_in[t][:, 1, :], xs[:, t, :], ACT.Square, accum_out=ss2[:, t:t + 1]).then_inc(squares, 1)
                act.wait_ge(mean_sq, NT + 1 + t + 1)
                act.activation(tmp3[:, t:t + 1], ss2[:, t:t + 1], ACT.Sqrt).then_inc(root, 1)

        @block.tensor
        def _(pe):
            def bank(fills, name):
                b, n = fills(name)
                if not (isinstance(n, int) and n == 0):
                    pe.wait_ge(work_free[b], n)
                return work(b), work_full[b]

            def matmuls(dst, lhs, rhs, n):
                for c in range(n):
                    last = pe.matmul(dst, lhs(c), rhs(c), start=(c == 0), stop=(c == n - 1))
                return last

            pre = PreFills()
            pe.wait_ge(consts, 1)
            for c in range(NK):
                w, full = bank(pre, "hT%d" % c)
                for t in range(NT):
                    if c == 0:
                        pe.wait_ge(x_normed, t + 1)
                    last = pe.transpose(w[:, t * P:(t + 1) * P], xn[:, t, c * P:(c + 1) * P], ident[:, :])
                last.then_inc(full, 1)
            pe.wait_ge(w_small_loaded, 32)
            for b in range(NK):
                pe.wait_ge(work_free[b], 1)

            def small(at, n):
                return lambda c: w_small[:, c, at - C_KC:at - C_KC + n]

            for name, at in (("kc", C_KC), ("vc", C_VC), ("ks", C_KS), ("kw", C_KW)):
                w, full = bank(pre, name)
                matmuls(w, small(at, P), lambda c: hT[:, c, :], NK).then_inc(full, 1)
            for name, src, n, tiles in (("vs", small(C_VS, P), P, range(NT)), ("vw0", small(C_VW, N_VW), N_VW, (0, 1)),
                                        ("vw1", small(C_VW, N_VW), N_VW, (2, 3))):
                w, full = bank(pre, name)
                for k, t in enumerate(tiles):
                    last = matmuls(w[:, k * n:(k + 1) * n], lambda c: hT[:, c, t * P:(t + 1) * P], src, NK)
                last.then_inc(full, 1)

            def project_gate(fills, name, b, n):
                w, full = bank(fills, name)
                matmuls(w, lambda c: w_gate[b][n][:, c, :], lambda c: hT[:, c, :], NK).then_inc(full, 1)

            def project_gates(c):
                pe.wait_ge(w_gate_loaded[c % 2], 32 * (c // 2) + 32)
                project_gate(pre, "gn%d" % c, c % 2, 0)
                project_gate(pre, "gf%d" % c, c % 2, 1)

            project_gates(0)
            w, full = bank(pre, "ffT")
            pe.wait_ge(lf_ready, 1)
            for t in range(NT):
                last = pe.transpose(w[0:NH, t * P:(t + 1) * P], lf[:, 2, t, :], ident[:, :])
            last.then_inc(full, 1)
            pe.wait_ge(consts, 3)

            def swapped(fills, names, src):
                for g, name in enumerate(names):
                    w, full = bank(fills, name)
                    pe.sem_inc(pe_took, 1)
                    pe.matmul(w[0:DH, :], swap[:, :], src[:, g, :], start=True, stop=True).then_inc(full, 1)

            pe.wait_ge(raw_k_ready, 2)
            swapped(pre, ("swks0", "swks1"), q_plain)
            swapped(pre, ("swkw0", "swkw1"), q_rope)
            project_gates(1)
            pe.wait_ge(w_cmp_loaded, 16 * 6)
            for k, name in enumerate(("hk", "hv")):
                w, full = bank(pre, name)
                n = G * NC
                dst = w[0:DH, 0:n].rearrange("p (g c) -> p g c", g=G)
                matmuls(dst, lambda l: w_c1[:, k, l, :],
                        lambda l: kv_c[:, k, :, 2 * l:2 * l + CS * (NC - 1) + 1:CS], CB // 2)
                matmuls(w[0:DH, n:n + 1], lambda l: w_c1[:, k, l, :], lambda l: pos_c[:, k, l:l + 1], CB // 2)\
                    .then_inc(full, 1)
            project_gates(2)
            w, full = bank(pre, "kcmp")
            pe.wait_ge(hid_ready, 2)
            pe.matmul(w[0:DH, 0:G * NC].rearrange("p (g c) -> p g c", g=G), w_c2[0:DH, 0, :], hid[:, 0, 0, :, :],
                      start=True, stop=True).then_inc(full, 1)
            w, full = bank(pre, "vcmp")
            for g in range(G):
                last = pe.matmul(w[0:NC, g * DH:(g + 1) * DH], hid[:, 0, 1, g, :], w_c2[0:DH, 1, :],
                                 start=True, stop=True)
            last.then_inc(full, 1)

            def project_q(fills, n):
                pe.wait_ge(w_q_loaded, n)
                w, full = bank(fills, "q")
                matmuls(w, lambda c: w_q[:, c, :], lambda c: hT[:, c, :], NK).then_inc(full, 1)

            project_q(pre, 32)
            project_gates(3)
            pe.wait_ge(q_ready, 1)
            swapped(pre, ("swq0", "swq1"), q_plain)

            def scored(u, h, q, k, rows):
                pe.wait_ge(half_free, u + 1)
                for t in (3, 2, 0, 1):
                    pe.matmul(scores(h, t), q[0:rows, t * P:(t + 1) * P], k[0:rows, 0:P * (t + 1)],
                              start=True, stop=True).then_inc(scores_ready, 1)

            def turned(u, h):
                pe.wait_ge(normed, 4 * u + 4)
                for k, blocks in enumerate(PT_FILLS):
                    for n, (kt, t) in enumerate(blocks):
                        last = pe.transpose(ps[:, 3 * h + k, n * P:(n + 1) * P],
                                            probs[:, h, P_OFF[t] + kt * P:P_OFF[t] + (kt + 1) * P], ident[:, :])
                    last.then_inc(turned_ready, 1)

            def valued(u, h, row, v, first, last):
                pe.wait_ge(pT_ready, 3 * u + 3)
                for n, kt in enumerate((0, 1, 2, 3)):
                    at = PT_OFF[kt] * P
                    ins = pe.matmul(o_bank[row:row + DH, kt * P:S], v(kt), pT[:, h, at:at + S - kt * P],
                                    start=(first and n == 0), stop=(last and n == 3))
                ins.then_inc(pT_free, 1)

            for b in range(BANKS):
                pe.wait_ge(work_free[b], (len(PRE) - b + BANKS - 1) // BANKS)
            pe.sem_inc(pT_free, 2)
            pe.sem_inc(pcT_used, 1)
            pe.wait_ge(rope_done, 3)
            pe.wait_ge(cmp_ready, 2)

            def part(fills, name, w_c, first, end):
                w, full = bank(fills, name) if first == 0 else (work(WORK), work_full[WORK])
                for c in range(first, end):
                    ins = pe.matmul(w, w_c(c), hT[:, c, :], start=(c == 0), stop=(c == NK - 1))
                if end == NK:
                    ins.then_inc(full, 1)

            def part_gate(fills, name, n, first, end):
                part(fills, name, lambda c: w_gate[0][n][:, c, :], first, end)

            def part_q(fills, loaded, first, end):
                if first == 0:
                    pe.wait_ge(w_q_loaded, loaded)
                part(fills, "q", lambda c: w_q[:, c, :], first, end)

            def nsa(i, last):
                f = Fills(N_NSA_LAST, NSA_LAST) if last else Fills(N_NSA, NSA_BODY, i)
                pe.wait_ge(rope_done, i + 3)
                w, full = bank(f, "cmp")
                for h in range(2):
                    for t in range(NT):
                        ins = pe.matmul(w[:, (h * NT + t) * NC:(h * NT + t + 1) * NC],
                                        q_plain[:, h, t * P:(t + 1) * P], kT_cmp[:, h, :], start=True, stop=True)
                ins.then_inc(full, 1)
                scored(4 * i, 0, q_rope[:, 0, :], kT_sel[:, 0, :], DH)
                scored(4 * i + 1, 1, q_rope[:, 0, :], kT_win[:, 0, :], DH)
                pe.wait_ge(w_gate_loaded[0], 32 * (GATES_PRE // 2) + 32 * i + 32)
                part_gate(f, "gn", 0, 0, 5)
                turned(4 * i, 0)
                part_gate(f, "gn", 0, 5, NK)
                pe.wait_ge(o_free, i + 1)
                valued(4 * i, 0, 0, lambda kt: v_sel[:, kt, 0:DH], True, False)
                scored(4 * i + 2, 0, q_rope[:, 1, :], kT_sel[:, 1, :], DH)
                if not last:
                    part_q(f, 32 * i + 64, 0, 5)
                turned(4 * i + 1, 1)
                if not last:
                    part_q(f, 0, 5, NK)
                valued(4 * i + 1, 1, 0, lambda kt: v_win[:, kt, 0:DH], False, False)
                scored(4 * i + 3, 1, q_rope[:, 1, :], kT_win[:, 1, :], DH)
                pe.wait_ge(cmp_masked, i + 1)
                for h in range(2):
                    w, full = bank(f, "pc%d" % h)
                    for t in range(NT):
                        ins = pe.transpose(w[0:NC, t * P:(t + 1) * P], pc[:, h, t, :], ident[:, :])
                    ins.then_inc(full, 1)
                part_gate(f, "gf", 1, 0, 5)
                pe.wait_ge(pcT_ready, 2 * i + 2)
                for h in range(2):
                    ins = pe.matmul(o_bank[h * DH:(h + 1) * DH, :], v_cmp[:, h, :], pcT[0:NC, h, :],
                                    start=(h == 1), stop=(h == 0))
                ins.then_inc(pcT_used, 1)
                turned(4 * i + 2, 0)
                part_gate(f, "gf", 1, 5, NK)
                valued(4 * i + 2, 0, DH, lambda kt: v_sel[:, kt, DH:P], False, False)
                if not last:
                    pe.wait_ge(q_ready, i + 2)
                    swapped(f, ("swq0", "swq1"), q_plain)
                turned(4 * i + 3, 1)
                valued(4 * i + 3, 1, DH, lambda kt: v_win[:, kt, DH:P], False, True)

            with pe.Fori(0, PAIRS - 1) as i:
                nsa(i, False)
            nsa(PAIRS - 1, True)

            def project_fox_qk(fills, n):
                pe.wait_ge(w_fqk_loaded, n)
                for part, name in enumerate(("fq", "fk")):
                    w, full = bank(fills, name)
                    matmuls(w, lambda c: w_fox[:, part, c, :], lambda c: hT[:, c, :], NK).then_inc(full, 1)

            def project_fox_v(fills, n):
                pe.wait_ge(w_fv_loaded, n)
                for k, name in enumerate(("fv0", "fv1")):
                    w, full = bank(fills, name)
                    for a in range(2):
                        t = 2 * k + a
                        last = matmuls(w[:, a * P:(a + 1) * P], lambda c: hT[:, c, t * P:(t + 1) * P],
                                       lambda c: w_fox[:, 2, c, :], NK)
                    last.then_inc(full, 1)

            project_fox_qk(Fills(N_FOX_PRE, FOX_BODY), 32)
            project_fox_v(Fills(N_FOX_PRE, FOX_BODY), 16)

            def fox(j, last):
                f = Fills(N_FOX, FOX_BODY, j)
                u = 4 * PAIRS + 2 * j
                pe.wait_ge(fox_qk_ready, j + 1)
                pe.wait_ge(decay_rows, 32 * j + 32)
                for h in range(2):
                    scored(u + h, h, q_fox[:, h, :], k_fox[:, h, :], DH + 2)
                if not last:
                    project_fox_qk(f, 32 * j + 64)
                pe.wait_ge(o_free, PAIRS + j + 1)
                pe.wait_ge(fox_v_ready, 2 * j + 2)
                for h in range(2):
                    turned(u + h, h)
                    valued(u + h, h, h * DH, lambda kt: v_fox[:, kt, h * DH:(h + 1) * DH], True, True)
                if not last:
                    project_fox_v(f, 16 * j + 32)

            with pe.Fori(0, PAIRS - 1) as j:
                fox(j, False)
            fox(PAIRS - 1, True)

            pe.wait_ge(half_free, 2 + 4 * PAIRS + 2 * PAIRS)
            pe.wait_ge(work_free[WORK], N_WORK)
            pe.wait_ge(o_free, 1 + 2 * PAIRS)
            pe.sem_inc(mix_used, 2)
            pe.sem_inc(mix_free, 2)
            with pe.Fori(0, NK // 2) as i:
                for b in range(2):
                    w = w_mix[b]
                    pe.wait_ge(w_mix_loaded[b], 48 * i + 48)
                    pe.wait_ge(mix_free, 2 * i + b + 1)
                    matmuls(ps[:, 4 * b + 2, :], lambda c: w["pn"][:, c, :], lambda c: oT_nsa[:, c, :], PAIRS)
                    matmuls(ps[:, 4 * b + 3, :], lambda c: w["pf"][:, c, :], lambda c: oT_fox[:, c, :], PAIRS)\
                        .then_inc(mix_full, 1)
            pe.wait_ge(mix_free, 2 + NK)
            pe.wait_ge(mix_used, 2 + NK)
            pe.wait_ge(w_o_loaded, 16 * NK)
            for k in range(NK):
                for t in range(NT):
                    for n in range(2):
                        ins = pe.matmul(ps[:, 2 * t + n, :], mixT[:, k, t * P:(t + 1) * P], w_o[k][:, n * 512:(n + 1) * 512],
                                        start=(k == 0), stop=(k == NK - 1))
                        if k == NK - 1:
                            ins.then_inc(out_full, 1)
            pe.wait_ge(x2_ready, 2 * NT)
            for c in range(NK):
                for t in range(NT):
                    if c == 0:
                        pe.wait_ge(xn2_ready, t + 1)
                    ins = pe.transpose(ps[:, c, t * P:(t + 1) * P], xn2[:, t, c * P:(c + 1) * P], ident[:, :])
                ins.then_inc(h2T_full, 1)
            pe.wait_ge(h2T_ready, NK)
            for t in range(NT):
                ins = matmuls(ps[:, 0, t * E:(t + 1) * E], lambda c: h2T[:, c, t * P:(t + 1) * P], lambda c: w_r[:, c, :], NK)
            ins.then_inc(logits_full, 1)
            pe.wait_ge(chosen_ready, 1)
            for t in range(NT + 1):
                dst = ps[:, 1, t * E:(t + 1) * E]
                for s in range(min(t, NT - 1) + 1):
                    last = s == min(t, NT - 1)
                    ins = pe.matmul(dst, earlier if s == t else ones, chosen[:, s, :], start=(s == 0), stop=last)
            ins.then_inc(pos_full, 1)
            pe.wait_ge(slots_loaded, 16)
            pe.transpose(ps[:, 2, 0:E], slots_sb, ident[0:E, 0:E]).then_inc(slots_turned, 1)
            pe.wait_ge(idx_ready, 2)
            pe.wait_ge(bias_ready, 2)
            pe.wait_ge(consts2, 9)

            def turn_x(e, b, k):
                pe.wait_ge(xg_loaded[b], 16 * k + 16)
                if not isinstance(e, int) or e > 1:
                    pe.wait_ge(gT_ready, 2 * e - 2)
                for n in range(2):
                    for c in range(4):
                        ins = pe.transpose(ps[:, 6 + n, c * P:(c + 1) * P], xg[b][:, (4 * n + c) * P:(4 * n + c + 1) * P],
                                           ident[:, :])
                    ins.then_inc(xT_full, 1)

            def up(e, b, k, picked, loaded, used):
                for n in range(4):
                    pe.matmul(ps[:, n, :], picked, bias[:, n * 512:(n + 1) * 512], start=True, stop=False)
                for c in range(NK):
                    loaded(c)
                    for n in range(4):
                        ins = pe.matmul(ps[:, n, :], xT[b][:, c, :], ring[:, c, n * 512:(n + 1) * 512],
                                        start=False, stop=(c == NK - 1))
                    used(c, ins)

            def down(b, picked, loaded, used):
                for n in range(2):
                    pe.matmul(ps[:, 4 + n, :], picked, bias[:, 2 * F + n * 512:2 * F + (n + 1) * 512],
                              start=True, stop=False)
                for c in range(NK):
                    if c % 2 == 0:
                        loaded(c // 2)
                    for n in range(2):
                        at = (c % 2) * D + n * 512
                        ins = pe.matmul(ps[:, 4 + n, :], gT[b][:, c, :], ring[:, NK + c // 2, at:at + 512],
                                        start=False, stop=(c == NK - 1))
                    if c % 2:
                        used(c // 2, ins)

            def turn_act(e):
                for n in range(2):
                    for c in range(4):
                        ins = pe.transpose(ps[:, 6 + n, c * P:(c + 1) * P], act_b[:, (4 * n + c) * P:(4 * n + c + 1) * P],
                                           ident[:, :])
                    ins.then_inc(gT_full, 1)

            def picks(e):
                return pick[:, e, :] if isinstance(e, int) else pick[:, bass.ds(e, 1), :].rearrange("p a m -> p (a m)")

            def expert(e, b, k, more, before):
                pe.wait_ge(xT_ready, 2 * e + 2)
                if before:
                    pe.wait_ge(hc_free, e)
                up(e, b, k, picks(e), lambda c: pe.wait_ge(slab_loaded[c], 16 * e + 16),
                   lambda c, ins: ins.then_inc(w1_used, 1))
                if more:
                    turn_x(e + 1, 1 - b, k + b)
                if before:
                    second(e - 1, 1 - b)
                if more:
                    pe.wait_ge(xT_ready, 2 * e + 4)
                pe.wait_ge(act_ready, e + 1)
                turn_act(e)

            def second(e, b):
                pe.wait_ge(gT_ready, 2 * e + 2)
                if not (isinstance(e, int) and e == 0):
                    pe.wait_ge(y_ready, e)
                down(b, picks(e), lambda s: pe.wait_ge(slab_loaded[NK + s], 16 * e + 16),
                     lambda s, ins: ins.then_inc(w2_used, 1))

            turn_x(0, 0, 0)
            expert(0, 0, 0, True, False)
            expert(1, 1, 0, True, True)
            expert(2, 0, 1, True, True)
            with pe.Fori(0, (E - 4) // 2) as i:
                expert(2 * i + 3, 1, i + 1, True, True)
                expert(2 * i + 4, 0, i + 2, True, True)
            expert(E - 1, 1, E // 2 - 1, False, True)
            second(E - 1, 1)

            pe.wait_ge(extra_ready, 1)
            pe.wait_ge(y_ready, E)
            total = pe.value_load(extra[0:1, 32:33], min_val=0, max_val=MAX_EXTRA)
            with pe.Fori(0, MAX_EXTRA) as o:
                with pe.If(total > o):
                    e = pe.value_load(extra[0:1, bass.ds(o, 1)], min_val=0, max_val=E - 1)
                    pe.wait_ge(ov_xg, 16 * o + 16)
                    for n in range(2):
                        for c in range(4):
                            ins = pe.transpose(ps[:, 6 + n, c * P:(c + 1) * P],
                                               xg[0][:, (4 * n + c) * P:(4 * n + c + 1) * P], ident[:, :])
                    ins.then_inc(ov_pe, 1)
                    pe.wait_ge(ov_dve, 4 * o + 1)
                    pe.wait_ge(ov_w, 192 * o + 192)
                    up(0, 0, 0, picks(e), lambda c: None, lambda c, ins: ins.then_inc(ov_pe, 1) if c == NK - 1 else None)
                    pe.wait_ge(ov_dve, 4 * o + 3)
                    for n in range(2):
                        for c in range(4):
                            ins = pe.transpose(ps[:, 6 + n, c * P:(c + 1) * P],
                                               act_b[:, (4 * n + c) * P:(4 * n + c + 1) * P], ident[:, :])
                    ins.then_inc(ov_pe, 1)
                    pe.wait_ge(ov_dve, 4 * o + 4)
                    down(0, picks(e), lambda s: None, lambda s, ins: ins.then_inc(ov_pe, 1) if s == 3 else None)
                    pe.wait_ge(ov_act, 2 * o + 4)

        @block.vector
        def _(dve):
            step = Steps(dve, dve_step)

            def take(semaphore, value):
                dve.wait_ge(semaphore, value)
                dve.sem_inc(dve_took, 1)

            def inverse_root(ss, r, t1, t2, count):
                step.link(dve.tensor_scalar(ss, ss, 1.0 / D, EPS, ALU.mult, ALU.add))
                dve.sem_inc(mean_sq, 1)
                dve.wait_ge(root, count)
                step.link(dve.reciprocal(r, t1))
                step.link(dve.tensor_tensor(t2, r, r, ALU.mult))
                step.link(dve.tensor_tensor(t2, t2, ss, ALU.mult))
                step.link(dve.tensor_scalar(t2, t2, -0.5, 1.5, ALU.mult, ALU.add))
                step.link(dve.tensor_tensor(r, r, t2, ALU.mult))

            for t in range(NT):
                dve.wait_ge(squares, t + 1)
                inverse_root(ss1[:, t:t + 1], rs1[:, t:t + 1], tmp1[:, t:t + 1], tmp2[:, t:t + 1], t + 1)
                dve.tensor_scalar(xn[:, t, :], xs[:, t, :], rs1[:, t:t + 1], None, ALU.mult).then_inc(x_normed, 1)

            dve.wait_ge(pos_loaded, 32)
            turns_, a0, posf = ang[:, 2, :], ang[:, 3, :], ang[:, 3, :]
            step.link(dve.tensor_copy(posf, pos_i))
            step.link(dve.tensor_scalar(a0, posf, freq[:, 0:1], None, ALU.mult))
            for k, shift in enumerate((0.0, 0.25)):
                step.link(dve.tensor_scalar(turns_, a0, 1.0 / TWO_PI, shift, ALU.mult, ALU.add))
                step.link(dve.tensor_scalar(turns_, turns_, MAGIC, -MAGIC, ALU.add, ALU.add))
                step.link(dve.scalar_tensor_tensor(ang[:, k, :], turns_, -PI1, a0, ALU.mult, ALU.add))
                step.link(dve.scalar_tensor_tensor(ang[:, k, :], turns_, -PI2, ang[:, k, :], ALU.mult, ALU.add))
                step.link(dve.scalar_tensor_tensor(ang[:, k, :], turns_, -PI3, ang[:, k, :], ALU.mult, ALU.add))
                step.link(dve.tensor_scalar(ang[:, k, :], ang[:, k, :], shift * TWO_PI, 3.1415925, ALU.add, ALU.min))
                step.link(dve.tensor_scalar(ang[:, k, :], ang[:, k, :], -3.1415925, None, ALU.max))
            dve.sem_inc(angles, 1)

            dve.wait_ge(small_loaded, 32)
            pre = PreFills()
            for c in range(1, NK, 2):
                b, n = pre("hT%d" % c)
                dve.wait_ge(work_full[b], n + 1)
                dve.tensor_scalar(hT[:, c, :], work(b), g1[:, c:c + 1], None, ALU.mult).then_inc(work_free[b], 1)

            for k in range(2):
                b, n = pre("vw%d" % k)
                dve.wait_ge(work_free[b], n + 1)
            step.link(dve.tensor_tensor(lf[:, 0, :, :], lf[:, 0, :, :],
                                        f_bias[:, :].unsqueeze(1).broadcast_to([P, NT, NH]), ALU.add))
            dve.scalar_tensor_tensor(lf[:, 1, :, :], lf[:, 0, :, :], -1.0, lf[:, 0, :, :], ALU.mult, ALU.max)\
               .then_inc(lf_abs, 1)
            dve.wait_ge(lf_ln, 1)
            dve.tensor_scalar(lf[:, 1, :, :], lf[:, 1, :, :], 1.0, None, ALU.add).then_inc(lf_abs, 1)
            dve.wait_ge(lf_ln, 2)
            dve.scalar_tensor_tensor(lf[:, 2, :, :], lf[:, 0, :, :], 0.0, lf[:, 1, :, :], ALU.min, ALU.subtract)\
               .then_inc(lf_ready, 1)
            dve.wait_ge(consts, 6)
            b, n = pre("ffT")
            dve.wait_ge(work_full[b], n + 1)
            dve.tensor_tensor_scan(decay[:, 0, :], ones8, work(b)[0:NH, :], 0.0, ALU.mult, ALU.add)\
               .then_inc(work_free[b], 1)
            dve.wait_ge(work_free[b], n + 1)
            dve.tensor_scalar(decay[:, 1, :], decay[:, 0, :], -1.0, None, ALU.mult).then_inc(decay_ready, 1)

            def rope(fills, names, dst):
                for g, name in enumerate(names):
                    b, n = fills(name)
                    dve.wait_ge(work_full[b], n + 1)
                    dve.tensor_tensor(dst[:, g, :], work(b)[0:DH, :], rope_sin[:, :], ALU.mult).then_inc(work_free[b], 1)
                    dve.wait_ge(work_free[b], n + 1)

            def rope_add(dst, count):
                dve.wait_ge(pool_rope, count)
                dve.tensor_tensor(dst, dst, ropeT, ALU.add).then_inc(rope_done, 1)

            dve.wait_ge(sines, 2)
            rope(pre, ("swks0", "swks1"), kT_sel)
            rope_add(kT_sel[:, :, :], 1)
            rope(pre, ("swkw0", "swkw1"), kT_win)
            rope_add(kT_win[:, :, :], 2)

            for k, name in enumerate(("hk", "hv")):
                b, n = pre(name)
                dve.wait_ge(work_full[b], n + 1)
                step.link(dve.tensor_copy(hbias[:, k:k + 1], work(b)[0:DH, G * NC:G * NC + 1]))
                z, t, a = (hid[:, m, k, :, :].rearrange("p g c -> p (g c)") for m in range(3))
                dve.tensor_scalar(z, work(b)[0:DH, 0:G * NC], hbias[:, k:k + 1], None, ALU.add).then_inc(work_free[b], 1)
                dve.wait_ge(work_free[b], n + 1)
                step.link(dve.tensor_tensor(t, z, z, ALU.mult))
                c1 = float(np.sqrt(2 / np.pi))
                step.link(dve.tensor_scalar(t, t, 0.044715 * c1, c1, ALU.mult, ALU.add))
                dve.tensor_tensor(t, t, z, ALU.mult).then_inc(hid_in, 1)
                step.link(dve.tensor_scalar(a, z, 0.5, None, ALU.mult))
                dve.wait_ge(hid_tanh, k + 1)
                dve.scalar_tensor_tensor(z, t, 1.0, a, ALU.add, ALU.mult).then_inc(hid_ready, 1)
            b, n = pre("kcmp")
            dve.wait_ge(work_full[b], n + 1)
            dve.tensor_copy(kT_cmp[:, :, :], work(b)[0:DH, 0:G * NC].rearrange("p (g c) -> p g c", g=G))\
               .then_inc(work_free[b], 1)
            b, n = pre("vcmp")
            dve.wait_ge(work_full[b], n + 1)
            dve.tensor_copy(v_cmp[:, :, :], work(b)[0:NC, 0:P].rearrange("p (g c) -> p g c", g=G))\
               .then_inc(work_free[b], 1)
            dve.wait_ge(work_free[b], n + 1)
            dve.sem_inc(cmp_ready, 2)
            rope(pre, ("swq0", "swq1"), q_rope)
            rope_add(q_rope, 3)

            def maxima(u, h):
                for t, n in ((3, 1), (2, 3), (0, 3), (1, 4)):
                    take(scores_ready, 4 * u + n)
                    dve.tensor_tensor_reduce(scores(h, t), scores(h, t), mask[:, S - P * (t + 1):S], 1.0, -3e38,
                                             ALU.add, ALU.max, mx[:, h, t:t + 1]).then_inc(dve_step, 1)
                step.n += NT
                dve.wait_ge(dve_step, step.turn + step.n)
                dve.tensor_scalar(ngm[:, h, :], mx[:, h, :], -1.0, None, ALU.mult).then_inc(max_ready, 1)

            def weights(u, h, gate):
                dve.wait_ge(probs_ready, 4 * u + 4)
                if gate is None:
                    dve.reciprocal(wts[:, h, :], sums[:, h, :]).then_inc(weights_ready, 1)
                    return
                step.link(dve.reciprocal(wts[:, h, :], sums[:, h, :]))
                dve.tensor_tensor(wts[:, h:h + 1, :], wts[:, h:h + 1, :], gate, ALU.mult).then_inc(weights_ready, 1)

            def take_pT(u, h):
                dve.wait_ge(pT_free, u + 1)
                at = 0
                for k, blocks in enumerate(PT_FILLS):
                    dve.wait_ge(turned_ready, 3 * u + k + 1)
                    m = len(blocks) * P
                    dve.tensor_copy(pT[:, h, at:at + m], ps[:, 3 * h + k, 0:m]).then_inc(pT_ready, 1)
                    at += m
                dve.wait_ge(pT_ready, 3 * u + 3)
                dve.sem_inc(half_free, 1)

            dve.wait_ge(consts, 5)

            def gate_of(i, h, branch):
                n = h * HPG * 3 + branch
                return gates[:, n + 3 * i:n + 3 * i + 1, :] if isinstance(i, int) else gates[:, bass.ds(3 * i + n, 1), :]

            def nsa(i, last):
                f = Fills(N_NSA_LAST, NSA_LAST) if last else Fills(N_NSA, NSA_BODY, i)
                b, n = f("cmp")
                dve.wait_ge(work_full[b], n + 1)
                dve.tensor_tensor(pc[:, :, :, :].rearrange("p h t c -> p (h t c)"), work(b)[:, 0:2 * NT * NC],
                                  cmp_neg[:, :, :, :].rearrange("p h t c -> p (h t c)"), ALU.add).then_inc(work_free[b], 1)
                dve.wait_ge(work_free[b], n + 1)
                step.link(dve.tensor_reduce(cmx, pc[:, :, :, :], AX.X, ALU.max))
                dve.tensor_tensor(pc[:, :, :, :], pc[:, :, :, :], cmx.unsqueeze(3).broadcast_to([P, 2, NT, NC]),
                                  ALU.subtract).then_inc(cmp_shifted, 1)
                maxima(4 * i, 0)
                maxima(4 * i + 1, 1)
                dve.wait_ge(cmp_exp, i + 1)
                step.link(dve.tensor_reduce(csum, pc[:, :, :, :], AX.X, ALU.add))
                step.link(dve.reciprocal(csum, csum))
                for h in range(2):
                    step.link(dve.tensor_tensor(csum[:, h:h + 1, :], csum[:, h:h + 1, :], gate_of(i, h, 0), ALU.mult))
                dve.tensor_tensor(pc[:, :, :, :], pc[:, :, :, :], csum.unsqueeze(3).broadcast_to([P, 2, NT, NC]),
                                  ALU.mult).then_inc(cmp_weighted, 1)
                weights(4 * i, 0, gate_of(i, 0, 1))
                take_pT(4 * i, 0)
                weights(4 * i + 1, 1, gate_of(i, 0, 2))
                maxima(4 * i + 2, 0)
                take_pT(4 * i + 1, 1)
                weights(4 * i + 2, 0, gate_of(i, 1, 1))
                maxima(4 * i + 3, 1)
                dve.wait_ge(pcT_used, i + 1)
                for h in range(2):
                    b, n = f("pc%d" % h)
                    dve.wait_ge(work_full[b], n + 1)
                    dve.tensor_copy(pcT[0:NC, h, :], work(b)[0:NC, :]).then_inc(work_free[b], 1)
                    dve.wait_ge(work_free[b], n + 1)
                    dve.sem_inc(pcT_ready, 1)
                take_pT(4 * i + 2, 0)
                weights(4 * i + 3, 1, gate_of(i, 1, 2))
                if not last:
                    rope(f, ("swq0", "swq1"), q_rope)
                    rope_add(q_rope, i + 4)
                take_pT(4 * i + 3, 1)

            with dve.Fori(0, PAIRS - 1) as i:
                step.enter(i, DVE_NSA)
                nsa(i, False)
                step.leave(PAIRS - 1)
            nsa(PAIRS - 1, True)

            def take_v(f):
                for k, name in enumerate(("fv0", "fv1")):
                    b, n = f(name)
                    dve.wait_ge(work_full[b], n + 1)
                    dve.tensor_copy(v_fox[:, 2 * k:2 * k + 2, :],
                                    work(b)[:, 0:2 * P].rearrange("p (t c) -> p t c", t=2)).then_inc(work_free[b], 1)
                    dve.wait_ge(work_free[b], n + 1)
                    dve.sem_inc(fox_v_ready, 1)

            take_v(Fills(N_FOX_PRE, FOX_BODY))

            def fox(j, last):
                f = Fills(N_FOX, FOX_BODY, j)
                u = 4 * PAIRS + 2 * j
                maxima(u, 0)
                maxima(u + 1, 1)
                for h in range(2):
                    weights(u + h, h, None)
                for h in range(2):
                    take_pT(u + h, h)
                if not last:
                    take_v(f)

            with dve.Fori(0, PAIRS - 1) as j:
                step.enter(j, DVE_FOX)
                fox(j, False)
                step.leave(PAIRS - 1)
            fox(PAIRS - 1, True)

            with dve.Fori(0, NK // 2) as i:
                for b in range(2):
                    take(mix_sig, 2 * i + b + 1)
                    dve.wait_ge(mix_full, 2 * i + b + 1)
                    dve.tensor_tensor(gate_sig[b], gate_sig[b], ps[:, 4 * b + 2:4 * b + 4, :], ALU.mult).then_inc(mix_free, 1)
                    dve.wait_ge(mix_free, 2 * i + b + 3)
                    dst = mixT[:, bass.ds(2 * i + b, 1), :].rearrange("p a s -> p (a s)")
                    dve.tensor_tensor(dst, gate_sig[b][:, 0, :], gate_sig[b][:, 1, :], ALU.add).then_inc(mix_used, 1)
            dve.wait_ge(bias_hi, 1)
            dve.tensor_tensor(b_raw, b_raw, bias[0:E, :], ALU.subtract).then_inc(bias_rest, 1)
            dve.wait_ge(bias_hi, 2)
            dve.tensor_tensor(b_raw, b_raw, b_mid, ALU.subtract).then_inc(bias_rest, 1)
            for t in range(NT):
                for n in range(2):
                    dve.wait_ge(out_full, 2 * t + n + 1)
                    sl = xs[:, t, n * 512:(n + 1) * 512]
                    dve.tensor_tensor(sl, sl, ps[:, 2 * t + n, :], ALU.add).then_inc(x2_ready, 1)
            dve.wait_ge(squares, 2 * NT)
            inverse_root(ss2, rs2, tmp3, tmp4, NT + 1)
            for t in range(NT):
                dve.tensor_scalar(xn2[:, t, :], xs[:, t, :], rs2[:, t:t + 1], None, ALU.mult).then_inc(xn2_ready, 1)
            dve.wait_ge(router_loaded, 48)
            for c in range(1, NK, 2):
                dve.wait_ge(h2T_full, c + 1)
                dve.tensor_scalar(h2T[:, c, :], ps[:, c, :], g2[:, c:c + 1], None, ALU.mult).then_inc(h2T_ready, 1)

            def each(v):
                return v.unsqueeze(2).broadcast_to([P, NT, E])

            def along(v):
                return v.unsqueeze(1).broadcast_to([P, NT, E])

            dve.wait_ge(consts2, 5)
            dve.wait_ge(logits_full, 1)
            step.link(dve.tensor_tensor(logit, ps[:, 0, 0:NT * E].rearrange("p (t e) -> p t e", t=NT), along(r_bias), ALU.add))
            for t in range(NT):
                step.link(dve.max(top8[:, t, :], logit[:, t, :]))
            fourth = top8[:, :, TOPK - 1]
            step.link(dve.tensor_tensor(over, logit, each(fourth), ALU.is_gt))
            step.link(dve.tensor_tensor(tied, logit, each(fourth), ALU.is_equal))
            dve.tensor_tensor(expd, logit, each(top8[:, :, 0]), ALU.subtract).then_inc(shifted, 1)
            step.link(dve.tensor_reduce(n_over, over, AX.X, ALU.add))
            step.link(dve.tensor_scalar(n_over, n_over, -1.0, float(TOPK), ALU.mult, ALU.add))
            for t in range(NT):
                step.link(dve.tensor_tensor_scan(run[:, t, :], one_e, tied[:, t, :], 0.0, ALU.mult, ALU.add))
            step.link(dve.tensor_tensor(run, run, each(n_over), ALU.is_le))
            step.link(dve.tensor_tensor(tied, tied, run, ALU.mult))
            dve.tensor_tensor(chosen, over, tied, ALU.add).then_inc(chosen_ready, 1)
            dve.wait_ge(chosen_ready, 1)
            for t in range(NT):
                step.link(dve.tensor_tensor_scan(rank[:, t, :], one_e, chosen[:, t, :], 0.0, ALU.mult, ALU.add))
            dve.wait_ge(pos_full, 1)
            step.link(dve.tensor_tensor(dest, ps[:, 1, 0:NT * E].rearrange("p (t e) -> p t e", t=NT), along(e_base), ALU.add))
            for k in range(TOPK):
                step.link(dve.scalar_tensor_tensor(hot, rank, float(k + 1), chosen, ALU.is_equal, ALU.mult))
                step.link(dve.tensor_tensor(prod, hot, dest, ALU.mult))
                step.link(dve.tensor_reduce(dest_k[:, k, :], prod, AX.X, ALU.add))
                dve.tensor_copy(dest_i[:, k, :], dest_k[:, k, :]).then_inc(dest_ready, 1)
            dve.wait_ge(expd_ready, 1)
            step.link(dve.tensor_tensor(expd, expd, chosen, ALU.mult))
            step.link(dve.tensor_reduce(r_sum, expd, AX.X, ALU.add))
            step.link(dve.reciprocal(r_sum, r_sum))
            step.link(dve.tensor_tensor(expd, expd, each(r_sum), ALU.mult))
            for k in range(TOPK):
                step.link(dve.scalar_tensor_tensor(hot, rank, float(k + 1), chosen, ALU.is_equal, ALU.mult))
                step.link(dve.tensor_tensor(prod, hot, expd, ALU.mult))
                step.link(dve.tensor_reduce(gate_k[:, k, :], prod, AX.X, ALU.add))
            count = ps[0:1, 1, NT * E:(NT + 1) * E]
            step.link(dve.tensor_scalar(many[0:1, :], count, float(P), None, ALU.is_gt))
            for m in (2, 3):
                step.link(dve.scalar_tensor_tensor(many[0:1, :], count, float(m * P), many[0:1, :], ALU.is_gt, ALU.add))
            step.link(dve.tensor_tensor_scan(cum[0:1, :], one_row[0:1, :], many[0:1, :], 0.0, ALU.mult, ALU.add))
            wide = [1, 16, E]
            step.link(dve.tensor_tensor(ov[0], cum[0:1, :].unsqueeze(1).broadcast_to(wide),
                                        ov_o.unsqueeze(2).broadcast_to(wide), ALU.is_le))
            step.link(dve.tensor_tensor(ov[1], ov[0], many[0:1, :].unsqueeze(1).broadcast_to(wide), ALU.mult))
            step.link(dve.tensor_reduce(ov_e, ov[0], AX.X, ALU.add))
            step.link(dve.tensor_reduce(ov_s, ov[1], AX.X, ALU.add))
            step.link(dve.tensor_tensor(ov_s, ov_o, ov_s, ALU.subtract))
            step.link(dve.tensor_scalar(ov_s, ov_s, float(P), float(P), ALU.mult, ALU.add))
            step.link(dve.tensor_copy(extra[:, 0:16], ov_e))
            step.link(dve.scalar_tensor_tensor(extra[:, 16:32], ov_e, float(S), ov_s, ALU.mult, ALU.add))
            dve.tensor_copy(extra[:, 32:33], cum[0:1, E - 1:E]).then_inc(extra_ready, 1)
            dve.wait_ge(slots_turned, 1)
            dve.tensor_copy(idx_y, ps[:, 2, 0:E]).then_inc(idx_ready, 1)
            dve.wait_ge(idx_ready, 1)
            dve.tensor_scalar(idx_x, idx_y, 2, None, ALU.logical_shift_right).then_inc(idx_ready, 1)

            def scaled(b, n, signal):
                dve.tensor_tensor(xT[b][:, 4 * n:4 * n + 4, :], ps[:, 6 + n, :].rearrange("p (c m) -> p c m", c=4),
                                  g2[:, 4 * n:4 * n + 4].unsqueeze(2).broadcast_to([P, 4, P]), ALU.mult).then_inc(signal, 1)

            def take_x(e, b):
                for n in range(2):
                    dve.wait_ge(xT_full, 2 * e + n + 1)
                    scaled(b, n, xT_ready)

            def clip():
                yield dve.tensor_scalar(gt_b, hc_g, LIMIT, None, ALU.min)
                yield dve.tensor_scalar(up_b, hc_u, LIMIT, -LIMIT, ALU.min, ALU.max)

            def expert(e, b, more):
                dve.wait_ge(w1_used, NK * e + NK)
                for ins, signal in zip(clip(), (gt_ready, hc_free)):
                    ins.then_inc(signal, 1)
                if more:
                    take_x(e + 1, 1 - b)
                dve.wait_ge(sg_ready, e + 1)
                dve.tensor_tensor(sg_b, sg_b, gt_b, ALU.mult).then_inc(glu_ready, 1)
                dve.wait_ge(glu_ready, e + 1)
                dve.wait_ge(hc_free, e + 1)
                dve.scalar_tensor_tensor(act_b, up_b, 1.0, sg_b, ALU.add, ALU.mult).then_inc(act_ready, 1)
                for n in range(2):
                    dve.wait_ge(gT_full, 2 * e + n + 1)
                    dve.tensor_copy(gT[b][:, 4 * n:4 * n + 4, :].rearrange("p c m -> p (c m)"), ps[:, 6 + n, :])\
                        .then_inc(gT_ready, 1)

            take_x(0, 0)
            expert(0, 0, True)
            with dve.Fori(0, E // 2 - 1) as i:
                expert(2 * i + 1, 1, True)
                expert(2 * i + 2, 0, True)
            expert(E - 1, 1, False)

            total = dve.value_load(extra[0:1, 32:33], min_val=0, max_val=MAX_EXTRA)
            dve.wait_ge(gT_ready, 2 * E)
            for b in range(2):
                dve.wait_ge(y_stored[b], 16 * E // 2)
            with dve.Fori(0, MAX_EXTRA) as o:
                with dve.If(total > o):
                    take(ov_over, o + 1)
                    dve.wait_ge(ov_idx, 16 * o + 16)
                    dve.tensor_copy(now_y[0], over_f).then_inc(ov_now, 1)
                    dve.wait_ge(ov_now, 2 * o + 1)
                    dve.tensor_scalar(now_x[0], now_y[0], 2, None, ALU.logical_shift_right).then_inc(ov_now, 1)
                    dve.wait_ge(ov_pe, 4 * o + 1)
                    for n in range(2):
                        scaled(0, n, ov_part)
                    dve.wait_ge(ov_part, 7 * o + 2)
                    dve.sem_inc(ov_dve, 1)
                    dve.wait_ge(ov_pe, 4 * o + 2)
                    for ins in clip():
                        ins.then_inc(ov_part, 1)
                    dve.wait_ge(ov_part, 7 * o + 4)
                    dve.sem_inc(ov_dve, 1)
                    dve.wait_ge(ov_act, 2 * o + 3)
                    dve.tensor_tensor(sg_b, sg_b, gt_b, ALU.mult).then_inc(ov_part, 1)
                    dve.wait_ge(ov_part, 7 * o + 5)
                    dve.scalar_tensor_tensor(act_b, up_b, 1.0, sg_b, ALU.add, ALU.mult).then_inc(ov_dve, 1)
                    dve.wait_ge(ov_pe, 4 * o + 3)
                    for n in range(2):
                        dve.tensor_copy(gT[0][:, 4 * n:4 * n + 4, :].rearrange("p c m -> p (c m)"), ps[:, 6 + n, :])\
                            .then_inc(ov_part, 1)
                    dve.wait_ge(ov_part, 7 * o + 7)
                    dve.sem_inc(ov_dve, 1)

            def summed(t):
                dve.wait_ge(y_loaded[t], 16)
                for k in range(TOPK):
                    ins = dve.scalar_tensor_tensor(xs[:, t, :], y_in[t][:, k, :], gate_k[:, k, t:t + 1], xs[:, t, :],
                                                   ALU.mult, ALU.add)
                    if k < TOPK - 1:
                        step.link(ins)
                    else:
                        ins.then_inc(sum_ready, 1)

            def finished(t):
                dve.wait_ge(squares, 2 * NT + t + 1)
                inverse_root(ss2[:, t:t + 1], rs2[:, t:t + 1], tmp3[:, t:t + 1], tmp4[:, t:t + 1], NT + 1 + t + 1)
                dve.scalar_tensor_tensor(y_in[t][:, 0, :], xs[:, t, :], rs2[:, t:t + 1], gf_b, ALU.mult, ALU.mult)\
                    .then_inc(result, 1)

            summed(0)
            dve.wait_ge(gf_loaded, 16)
            for t in range(1, NT):
                summed(t)
                finished(t - 1)
            finished(NT - 1)


_INS = ["x", "positions", "norm1_g", "w_in", "cmp_pos_emb", "cmp_w1", "cmp_w2", "fox_f_bias", "w_proj_nsa",
        "w_proj_fox", "w_out", "norm2_g", "router_w", "router_b", "expert_w1", "expert_b1", "expert_w2",
        "expert_b2", "norm_f_g"]


def kernel(**inputs):
    import concourse.bacc as bacc
    from concourse.bass_utils import run_bass_kernel_spmd

    nc = bacc.Bacc("TRN2", target_bir_lowering=False, num_devices=1)
    arrays = {n: np.ascontiguousarray(inputs[n]) for n in _INS}
    freqs = np.zeros((DH, 1), np.float32)
    freqs[:ROT, 0] = np.tile(500000.0 ** (-np.arange(0, ROT, 2) / ROT), 2).astype(np.float32)
    arrays["rope_freqs"] = freqs
    args = [nc.dram_tensor("in_" + n, a.shape, mybir.dt.from_np(a.dtype), kind="ExternalInput").ap()
            for n, a in arrays.items()]
    out = nc.dram_tensor("out_0", (1, S, D), F32, kind="ExternalOutput").ap()
    hybrid_block(nc, *args, out)
    r = run_bass_kernel_spmd(nc, [{"in_" + n: a for n, a in arrays.items()}], core_ids=[0])
    return r.results[0]["out_0"]
```
